# Optimizing a Trainium2 kernel written in Bass

```python
import jax, jax.numpy as jnp
from jax import lax
import numpy as np

D_MODEL = 1024
BATCH = 1
SEQ = 1024
DEPTH = 1
DEC_BATCH = 8
DEC_SEQ = 16
PAST_LEN = 512

CHUNK = 64
N_MEM = 256
FOX_HEAD_DIM = 64
FOX_HEADS = D_MODEL // 128
FOX_WIDTH = FOX_HEADS * FOX_HEAD_DIM
POOL_WINDOWS = (2, 4, 8, 16)
POOL_GROUPS = 4
POOL_WIDTH = D_MODEL // 2
POOL_GROUP_DIM = POOL_WIDTH // POOL_GROUPS
POOL_HIST = 15
MEM_HEADS = 4
MEM_WIDTH = D_MODEL // 2
MEM_HEAD_DIM = MEM_WIDTH // MEM_HEADS
N_BRANCH = 3
D_FF = 4 * D_MODEL
Q_BLOCK = 128
EPS = 1e-6
FORGET_BIAS = 2.0
SPLIT_SIZES = (FOX_WIDTH, FOX_WIDTH, FOX_WIDTH, FOX_HEADS, POOL_WIDTH, MEM_WIDTH, N_BRANCH * D_MODEL)
IN_DIM = 3 * FOX_WIDTH + FOX_HEADS + POOL_WIDTH + MEM_WIDTH + N_BRANCH * D_MODEL

kernel_name = 'fox_pool_memory_hybrid_stream_step'

def _rmsnorm(x, g):
    xf = x.astype(jnp.float32)
    y = xf * lax.rsqrt(jnp.mean(xf * xf, axis=-1, keepdims=True) + EPS)
    return (y * g.astype(jnp.float32)).astype(x.dtype)

def _split_points():
    return np.cumsum(SPLIT_SIZES)[:-1].tolist()

def _in_proj(x, g, w_in, b_f):
    B, T, _ = x.shape
    z = _rmsnorm(x, g) @ w_in
    q, k, v, f, u, qm, gates = jnp.split(z, _split_points(), axis=-1)
    logf = jax.nn.log_sigmoid((f + b_f).astype(jnp.float32))
    q = q.reshape(B, T, FOX_HEADS, FOX_HEAD_DIM)
    k = k.reshape(B, T, FOX_HEADS, FOX_HEAD_DIM)
    v = v.reshape(B, T, FOX_HEADS, FOX_HEAD_DIM)
    qm = qm.reshape(B, T, MEM_HEADS, MEM_HEAD_DIM)
    return q, k, v, logf, u, qm, gates

def _fox_attend(q, k, v, cq, ck, qpos, kpos):
    scale = FOX_HEAD_DIM ** -0.5
    s = jnp.einsum('bqhd,bkhd->bhqk', q.astype(jnp.float32), k.astype(jnp.float32)) * scale
    s = s + jnp.transpose(cq, (0, 2, 1))[:, :, :, None] - jnp.transpose(ck, (0, 2, 1))[:, :, None, :]
    s = jnp.where(kpos[None, :] <= qpos[:, None], s, -jnp.inf)
    p = jax.nn.softmax(s, axis=-1)
    o = jnp.einsum('bhqk,bkhd->bqhd', p, v.astype(jnp.float32))
    return o.astype(q.dtype)

def _fox_prompt(q, k, v, logf):
    B, S, H, Dh = q.shape
    c = jnp.cumsum(logf, axis=1)
    kpos = jnp.arange(S)

    def block(i):
        start = i * Q_BLOCK
        qb = lax.dynamic_slice_in_dim(q, start, Q_BLOCK, axis=1)
        cqb = lax.dynamic_slice_in_dim(c, start, Q_BLOCK, axis=1)
        qpos = start + jnp.arange(Q_BLOCK)
        return _fox_attend(qb, k, v, cqb, c, qpos, kpos)

    out = lax.map(block, jnp.arange(S // Q_BLOCK))
    return jnp.transpose(out, (1, 0, 2, 3, 4)).reshape(B, S, H, Dh)

def _pool_mix(u_ext, pos0, w_pool, s_pool):
    B, L, _ = u_ext.shape
    T = L - POOL_HIST
    uf = u_ext.astype(jnp.float32).reshape(B, L, POOL_GROUPS, POOL_GROUP_DIM)
    cs = jnp.concatenate([jnp.zeros((B, 1, POOL_GROUPS, POOL_GROUP_DIM), jnp.float32),
                          jnp.cumsum(uf, axis=1)], axis=1)
    end = cs[:, POOL_HIST + 1:]
    pos = pos0 + jnp.arange(T)
    means = []
    for g, w in enumerate(POOL_WINDOWS):
        start = cs[:, POOL_HIST + 1 - w: POOL_HIST + 1 - w + T, g]
        cnt = jnp.minimum(w, pos + 1).astype(jnp.float32)
        means.append((end[:, :, g] - start) / cnt[None, :, None])
    pooled = jnp.stack(means, axis=2) - uf[:, POOL_HIST:]
    mixed = jnp.einsum('btgc,gcd->btgd', pooled, w_pool.astype(jnp.float32))
    mixed = mixed * s_pool.astype(jnp.float32).reshape(POOL_GROUPS, POOL_GROUP_DIM)
    return mixed.reshape(B, T, POOL_WIDTH).astype(u_ext.dtype)

def _mem_kv(mem, g, w_mkv):
    B, M, _ = mem.shape
    kv = _rmsnorm(mem, g) @ w_mkv
    mk, mv = jnp.split(kv, 2, axis=-1)
    return (mk.reshape(B, M, MEM_HEADS, MEM_HEAD_DIM), mv.reshape(B, M, MEM_HEADS, MEM_HEAD_DIM))

def _mem_attend(qm, mk, mv):
    scale = MEM_HEAD_DIM ** -0.5
    s = jnp.einsum('bqhd,bmhd->bhqm', qm.astype(jnp.float32), mk.astype(jnp.float32)) * scale
    p = jax.nn.softmax(s, axis=-1)
    return jnp.einsum('bhqm,bmhd->bqhd', p, mv.astype(jnp.float32)).astype(qm.dtype)

def _merge(x, o_fox, o_pool, o_mem, gates, w_br_fox, w_br_pool, w_br_mem, w_out):
    B, T, _ = x.shape
    g = jax.nn.sigmoid(gates.astype(jnp.float32)).astype(x.dtype).reshape(B, T, N_BRANCH, D_MODEL)
    m = (g[:, :, 0] * (o_fox.reshape(B, T, FOX_WIDTH) @ w_br_fox)
         + g[:, :, 1] * (o_pool @ w_br_pool)
         + g[:, :, 2] * (o_mem.reshape(B, T, MEM_WIDTH) @ w_br_mem))
    return x + m @ w_out

def _ffn(h, g, w_up, w_down):
    a = jax.nn.relu(_rmsnorm(h, g) @ w_up)
    return h + (a * a) @ w_down

def setup_inputs(seed: int = 0) -> dict:
    key = jax.random.key(seed)
    ks = jax.random.split(key, 24)

    def nrm(k, shape, scale=1.0):
        return scale * jax.random.normal(k, shape, jnp.float32)

    D = D_MODEL
    return {
        'x_prompt': nrm(ks[0], (BATCH, SEQ, D)),
        'x_sample': nrm(ks[1], (DEC_BATCH, DEC_SEQ, D)),
        'mem_prompt': nrm(ks[2], (BATCH, N_MEM, D)),
        'cache_fox_k': nrm(ks[3], (DEPTH, DEC_BATCH, PAST_LEN, FOX_HEADS, FOX_HEAD_DIM)),
        'cache_fox_v': nrm(ks[4], (DEPTH, DEC_BATCH, PAST_LEN, FOX_HEADS, FOX_HEAD_DIM)),
        'cache_fox_logf': jax.nn.log_sigmoid(FORGET_BIAS + nrm(ks[5], (DEPTH, DEC_BATCH, PAST_LEN, FOX_HEADS), 0.5)),
        'cache_pool': nrm(ks[6], (DEPTH, DEC_BATCH, POOL_HIST, POOL_WIDTH)),
        'cache_mem_k': nrm(ks[7], (DEPTH, DEC_BATCH, N_MEM, MEM_HEADS, MEM_HEAD_DIM)),
        'cache_mem_v': nrm(ks[8], (DEPTH, DEC_BATCH, N_MEM, MEM_HEADS, MEM_HEAD_DIM)),
        'g_attn': 1.0 + nrm(ks[9], (DEPTH, D), 0.1),
        'w_in': nrm(ks[10], (DEPTH, D, IN_DIM), D ** -0.5),
        'b_f': FORGET_BIAS + nrm(ks[11], (DEPTH, FOX_HEADS), 0.1),
        'w_pool': nrm(ks[12], (DEPTH, POOL_GROUPS, POOL_GROUP_DIM, POOL_GROUP_DIM), POOL_GROUP_DIM ** -0.5),
        's_pool': 1.0 + nrm(ks[13], (DEPTH, POOL_WIDTH), 0.1),
        'g_mem': 1.0 + nrm(ks[14], (DEPTH, D), 0.1),
        'w_mkv': nrm(ks[15], (DEPTH, D, 2 * MEM_WIDTH), D ** -0.5),
        'w_br_fox': nrm(ks[16], (DEPTH, FOX_WIDTH, D), FOX_WIDTH ** -0.5),
        'w_br_pool': nrm(ks[17], (DEPTH, POOL_WIDTH, D), POOL_WIDTH ** -0.5),
        'w_br_mem': nrm(ks[18], (DEPTH, MEM_WIDTH, D), MEM_WIDTH ** -0.5),
        'w_out': nrm(ks[19], (DEPTH, D, D), D ** -0.5),
        'g_mlp': 1.0 + nrm(ks[20], (DEPTH, D), 0.1),
        'w_up': nrm(ks[21], (DEPTH, D, D_FF), D ** -0.5),
        'w_down': nrm(ks[22], (DEPTH, D_FF, D), D_FF ** -0.5),
        'g_final': 1.0 + nrm(ks[23], (D,), 0.1),
    }

def reference(x_prompt, x_sample, mem_prompt, cache_fox_k, cache_fox_v, cache_fox_logf, cache_pool,
              cache_mem_k, cache_mem_v, g_attn, w_in, b_f, w_pool, s_pool, g_mem, w_mkv,
              w_br_fox, w_br_pool, w_br_mem, w_out, g_mlp, w_up, w_down, g_final):
    xp, xs = x_prompt, x_sample
    B = xp.shape[0]
    T = xs.shape[1]
    P = cache_fox_k.shape[2]
    fk_p, fv_p, fl_p, pl_p, mk_p, mv_p = [], [], [], [], [], []
    fk_s, fv_s, fl_s, pl_s = [], [], [], []
    for l in range(DEPTH):
        q, k, v, logf, u, qm, gates = _in_proj(xp, g_attn[l], w_in[l], b_f[l])
        o_fox = _fox_prompt(q, k, v, logf)
        u_ext = jnp.concatenate([jnp.zeros((B, POOL_HIST, POOL_WIDTH), u.dtype), u], axis=1)
        o_pool = _pool_mix(u_ext, 0, w_pool[l], s_pool[l])
        mk, mv = _mem_kv(mem_prompt, g_mem[l], w_mkv[l])
        o_mem = _mem_attend(qm, mk, mv)
        h = _merge(xp, o_fox, o_pool, o_mem, gates, w_br_fox[l], w_br_pool[l], w_br_mem[l], w_out[l])
        xp = _ffn(h, g_mlp[l], w_up[l], w_down[l])
        fk_p.append(k); fv_p.append(v); fl_p.append(logf)
        pl_p.append(u_ext[:, -POOL_HIST:]); mk_p.append(mk); mv_p.append(mv)

        q, k, v, logf, u, qm, gates = _in_proj(xs, g_attn[l], w_in[l], b_f[l])
        k_all = jnp.concatenate([cache_fox_k[l].astype(k.dtype), k], axis=1)
        v_all = jnp.concatenate([cache_fox_v[l].astype(v.dtype), v], axis=1)
        logf_all = jnp.concatenate([cache_fox_logf[l].astype(jnp.float32), logf], axis=1)
        c_all = jnp.cumsum(logf_all, axis=1)
        o_fox = _fox_attend(q, k_all, v_all, c_all[:, P:], c_all, P + jnp.arange(T), jnp.arange(P + T))
        u_ext = jnp.concatenate([cache_pool[l].astype(u.dtype), u], axis=1)
        o_pool = _pool_mix(u_ext, P, w_pool[l], s_pool[l])
        o_mem = _mem_attend(qm, cache_mem_k[l], cache_mem_v[l])
        h = _merge(xs, o_fox, o_pool, o_mem, gates, w_br_fox[l], w_br_pool[l], w_br_mem[l], w_out[l])
        xs = _ffn(h, g_mlp[l], w_up[l], w_down[l])
        fk_s.append(k); fv_s.append(v); fl_s.append(logf); pl_s.append(u_ext[:, -POOL_HIST:])

    y_prompt = _rmsnorm(xp, g_final)
    y_sample = _rmsnorm(xs, g_final)
    new_fox_k_p = jnp.stack(fk_p)
    new_fox_v_p = jnp.stack(fv_p)
    new_fox_logf_p = jnp.stack(fl_p)
    new_pool_p = jnp.stack(pl_p)
    new_mem_k_p = jnp.stack(mk_p)
    new_mem_v_p = jnp.stack(mv_p)
    new_fox_k_s = jnp.stack(fk_s)
    new_fox_v_s = jnp.stack(fv_s)
    new_fox_logf_s = jnp.stack(fl_s)
    new_pool_s = jnp.stack(pl_s)
    return (y_prompt, y_sample, new_fox_k_p, new_fox_v_p, new_fox_logf_p, new_pool_p, new_mem_k_p, new_mem_v_p,
            new_fox_k_s, new_fox_v_s, new_fox_logf_s, new_pool_s)


_drawn_inputs = setup_inputs


def setup_inputs(seed=0):
    import zlib

    import numpy as np

    out = dict(_drawn_inputs(seed))
    spreads = {}
    factors = {}
    for name, (base, spread) in spreads.items():
        noise = np.random.default_rng([zlib.crc32(name.encode()), seed]).standard_normal(out[name].shape)
        drawn = base * np.exp(spread * noise) if base else spread * noise
        out[name] = __import__('jax').numpy.asarray(drawn.astype(out[name].dtype))
    for name, factor in factors.items():
        out[name] = (out[name] * factor).astype(out[name].dtype)
    return out
```

```python
from contextlib import ExitStack

import concourse.bass as bass
from concourse import mybir

ALU = mybir.AluOpType
ACT = mybir.ActivationFunctionType
F32 = mybir.dt.float32
F32R = mybir.dt.float32r
AX_X = mybir.AxisListType.X
ds = bass.ds

P = 128
BIG = 2.0 ** 127
EPS = 1e-6
COMBOS = ((0, 0), (0, 1), (1, 0))


def encoder_program(nc, x_prompt, x_sample, mem_prompt, cache_fox_k, cache_fox_v, cache_fox_logf, cache_pool,
                    cache_mem_k, cache_mem_v, g_attn, w_in, b_f, w_pool, s_pool, g_mem, w_mkv,
                    w_br_fox, w_br_pool, w_br_mem, w_out, g_mlp, w_up, w_down, g_final,
                    y_prompt, y_sample, new_fox_k_p, new_fox_v_p, new_fox_logf_p, new_pool_p, new_mem_k_p,
                    new_mem_v_p, new_fox_k_s, new_fox_v_s, new_fox_logf_s, new_pool_s):
    D = x_prompt.shape[2]
    SEQ = x_prompt.shape[1]
    NB, NQ = x_sample.shape[0], x_sample.shape[1]
    PAST = cache_fox_k.shape[2]
    FH, FD = cache_fox_k.shape[3], cache_fox_k.shape[4]
    MH, MD = cache_mem_k.shape[3], cache_mem_k.shape[4]
    NMEM = mem_prompt.shape[1]
    FW = FH * FD
    PW = cache_pool.shape[3]
    HIST = cache_pool.shape[2]
    DFF = w_up.shape[2]
    KT = D // P
    BT = FW // P
    QT = SEQ // P
    NT = QT + 1
    T = NT * P
    TB = T // 3
    MT = NMEM // P
    ST = PAST // P
    FT = DFF // P
    CH = 4
    NCH = FT // CH
    assert NB * NQ == P and FH * NQ == P and FW == PW == MH * MD == 512 and T == 3 * TB
    C_F = 3 * FW
    C_U = C_F + FH
    C_QM = C_U + PW
    C_G = C_QM + MH * MD

    uses, at = {}, [0, 0]
    for name, n0, n1 in (("forget", 0, 1), ("fox", 2 * BT, BT), ("merge0", KT, KT), ("pool", 2, 2),
                         ("merge1", KT, KT), ("mem", 2 * BT, BT), ("merge2", KT, KT),
                         ("out", KT // 2, KT // 2), ("ffn", NCH * (CH + KT) // 2, NCH * (CH + KT) // 2)):
        uses[name] = tuple(at)
        at[0] += n0
        at[1] += n1

    rows = lambda w: w.rearrange("a (k p) n -> p (a k) n", p=P)
    win, wmkv, wout, wup, wdown = rows(w_in), rows(w_mkv), rows(w_out), rows(w_up), rows(w_down)
    wbr = [rows(w_br_fox), rows(w_br_pool), rows(w_br_mem)]
    xp_rows = x_prompt.rearrange("a (t p) d -> p (a t) d", p=P)
    xs_rows = x_sample.rearrange("b q d -> (b q) d")
    mem_rows = mem_prompt.rearrange("a (t p) d -> p (a t) d", p=P)
    kp_out = new_fox_k_p.rearrange("l a (t p) h d -> p (l a t) (h d)", p=P)
    vp_out = new_fox_v_p.rearrange("l a (t p) h d -> p (l a t) (h d)", p=P)
    ks_out = new_fox_k_s.rearrange("l b q h d -> (l b q) (h d)")
    vs_out = new_fox_v_s.rearrange("l b q h d -> (l b q) (h d)")
    mk_out = new_mem_k_p.rearrange("l a (t p) h d -> p (l a t) (h d)", p=P)
    mv_out = new_mem_v_p.rearrange("l a (t p) h d -> p (l a t) (h d)", p=P)
    negc_p = nc.dram_tensor("negc_prompt", (FH // 2, 2 * SEQ), F32, kind="Internal").ap()
    negc_s = nc.dram_tensor("negc_sample", (NB * FH * NQ, PAST + NQ), F32, kind="Internal").ap()

    with ExitStack() as ctx:
        def sem(name):
            return ctx.enter_context(nc.semaphore(name))

        def tensor(scope, name, shape, dt=F32):
            return scope.enter_context(nc.sbuf_tensor(name, shape, dt))

        def parts(scope, name, shape):
            return [tensor(scope, f"{name}_{x}", shape, F32R) for x in ("hi", "lo")]

        ps = ctx.enter_context(nc.psum_tensor("ps", [P, 8, 512], F32))

        def pset(k):
            return ps[:, 3 * k:3 * k + 3, 0:TB]

        A = parts(ctx, "act", [P, KT, T])
        O = parts(ctx, "branch", [P, BT, T])
        w_raw = [tensor(ctx, f"w_raw{k}", [P, KT, P]) for k in range(2)]
        W = [parts(ctx, f"w{k}", [P, KT, P]) for k in range(2)]
        ident = tensor(ctx, "ident", [P, P])
        ident_r = tensor(ctx, "ident_r", [P, P], F32R)
        causal_r = tensor(ctx, "causal_r", [P, P], F32R)
        rsel = tensor(ctx, "rsel", [P, NQ])
        mask_new = tensor(ctx, "mask_new", [P, NQ])
        eps_t = tensor(ctx, "eps_t", [P, 1])
        s_col = tensor(ctx, "s_col", [P, BT])
        g_col = tensor(ctx, "g_col", [P, KT])
        cnt_col = tensor(ctx, "cnt_col", [P, 16])
        small = tensor(ctx, "small", [P, 16])
        MX, NM, SUM, RC = [[small[:, 4 * i + k:4 * i + k + 1] for k in range(2)] for i in range(4)]

        def scoped(build):
            with ExitStack() as scope:
                return build(scope)

        def norm_buffers(scope, tag):
            return dict(x_in=[tensor(scope, f"{tag}_in{k}", [P, D]) for k in range(2)],
                        xs=[tensor(scope, f"{tag}_xs{k}", [P, D]) for k in range(2)],
                        junk=tensor(scope, f"{tag}_sq", [P, D]), g=tensor(scope, f"{tag}_g", [P, D]))

        def forget_buffers(scope):
            return dict(x=tensor(scope, "f_x", [FH, T]), e=tensor(scope, "f_e", [FH, T]),
                        nl=tensor(scope, "f_nl", [FH, T]), zero=tensor(scope, "f_zero", [NB * FH, SEQ]),
                        c=tensor(scope, "f_c", [FH, SEQ]), cs=tensor(scope, "f_cs", [NB * FH, PAST + NQ]),
                        ext=tensor(scope, "f_ext", [NB * FH, PAST + NQ]),
                        cache=tensor(scope, "f_cache", [P, ST, NB * FH]), bf=tensor(scope, "f_b", [FH, 1]),
                        tok=tensor(scope, "f_tok", [P, NT, FH]), m3=tensor(scope, "f_m3", [P, NB, NQ]),
                        m4=tensor(scope, "f_m4", [P, NB, NQ]), cm=tensor(scope, "f_cm", [P, P]))

        def attention_buffers(scope, tag, kv_tiles, keys, bias):
            b = dict(q=parts(scope, f"{tag}_q", [P, T]), k=parts(scope, f"{tag}_k", [P, kv_tiles * P]),
                     kf=tensor(scope, f"{tag}_kf", [P, kv_tiles * P]),
                     vf=tensor(scope, f"{tag}_vf", [P, kv_tiles * P]),
                     ktok=tensor(scope, f"{tag}_ktok", [P, kv_tiles, P]),
                     vtok=tensor(scope, f"{tag}_vtok", [P, kv_tiles, P]),
                     v=parts(scope, f"{tag}_v", [P, kv_tiles, P]),
                     p=[tensor(scope, f"{tag}_p{k}", [P, keys]) for k in range(2)],
                     pt=parts(scope, f"{tag}_pt", [P, keys // P, 2 * P]))
            if bias:
                b["negc"] = tensor(scope, f"{tag}_negc", [P, 2, keys])
            return b

        def sample_buffers(scope, tag, tiles, new):
            heads = FH if new else MH
            b = dict(kraw=tensor(scope, f"{tag}_kraw", [P, tiles, 512]),
                     vraw=tensor(scope, f"{tag}_vraw", [P, tiles, 512]),
                     kt=parts(scope, f"{tag}_kt", [P, 4, tiles * P]),
                     v=parts(scope, f"{tag}_v", [P, tiles, 512]),
                     qpad=parts(scope, f"{tag}_qpad", [P, 4 * (P + NQ * heads // 4)]),
                     p=tensor(scope, f"{tag}_p", [P, tiles * P + NQ]),
                     pt=parts(scope, f"{tag}_pt", [P, tiles + 1, P]),
                     om=tensor(scope, f"{tag}_om", [P, 512]), block=tensor(scope, f"{tag}_block", [P, 512]))
            if new:
                b["bias"] = tensor(scope, f"{tag}_bias", [P, tiles * P + NQ])
                b["vnraw"] = tensor(scope, f"{tag}_vnraw", [NQ, 512])
                b["vn"] = parts(scope, f"{tag}_vn", [NQ, 512])
            return b

        bn = scoped(lambda s: norm_buffers(s, "xn"))
        bf = scoped(forget_buffers)
        with ExitStack() as scope:
            QS = parts(scope, "qs", [P, BT, P])
            KS = parts(scope, "ks", [P, BT, P])
            fx = scoped(lambda s: attention_buffers(s, "fox", NT, SEQ, True))
            sf = scoped(lambda s: sample_buffers(s, "foxs", ST, True))
        H = tensor(ctx, "h", [P, KT, T])

        def merge_buffers(scope):
            return dict(gate=tensor(scope, "gate", [P, T]), prod=tensor(scope, "prod", [P, T]))

        mg = scoped(merge_buffers)
        UL = P // NB * 2
        UW = 16 + SEQ + NB * UL

        def pool_buffers(scope):
            return dict(u=[tensor(scope, f"u{k}", [P, UW]) for k in range(3)], pooled=tensor(scope, "pooled", [P, T]),
                        hist=tensor(scope, "pool_hist", [NB * HIST, PW]),
                        wraw=tensor(scope, "wpool_raw", [P, BT, P]), w=parts(scope, "wpool", [P, BT, P]),
                        tail=tensor(scope, "pool_tail", [P, 2, PW]), uf=tensor(scope, "pool_uf", [P, 2 * P]))

        pb = scoped(pool_buffers)
        with ExitStack() as scope:
            MQS = parts(scope, "mqs", [P, BT, P])
            with ExitStack() as inner:
                ME = parts(inner, "memn", [P, KT, NMEM])
                with ExitStack() as innermost:
                    bm = norm_buffers(innermost, "mn")
                mx = attention_buffers(inner, "mem", MT, NMEM, False)
            sm = sample_buffers(scope, "mems", MT, False)

        def out_buffers(scope):
            return dict(xt=[tensor(scope, f"xt{k}", [P, T]) for k in range(2)],
                        xtok=[tensor(scope, f"xtok{k}", [P, NT, P]) for k in range(2)],
                        sq=tensor(scope, "h_sq", [P, T]), acc=tensor(scope, "h_acc", [P, T]),
                        ones=tensor(scope, "ones", [P, P]), hn=tensor(scope, "hn", [P, T]))

        with ExitStack() as scope:
            ob = out_buffers(scope)
            fb = dict(r=tensor(scope, "ff_r", [P, T]), a=tensor(scope, "ff_a", [P, T]))
        yb = scoped(lambda s: dict(g=tensor(s, "gfin", [P, D]), junk=tensor(s, "fin_sq", [P, D]),
                                   y=[tensor(s, f"fin_y{k}", [P, D]) for k in range(2)],
                                   st=[tensor(s, f"fin_st{k}", [P, 4]) for k in range(2)]))

        consts_made = sem("consts_made")
        consts_step = sem("consts_step")
        consts_in = sem("consts_in")
        raw_full = [sem(f"raw_full{k}") for k in range(2)]
        w_hi = [sem(f"w_hi{k}") for k in range(2)]
        w_lo = [sem(f"w_lo{k}") for k in range(2)]
        gemm_over = [sem(f"gemm_over{k}") for k in range(2)]
        evacuated = [sem(f"evacuated{k}") for k in range(2)]
        sp_passed = sem("sp_passed")
        phase_over = sem("phase_over")

        def group(tag, *names):
            return {n: sem(f"{tag}_{n}") for n in names}

        def next_phase(eng, number, wait=True):
            eng.drain().then_inc(phase_over, 1)
            if wait:
                eng.wait_ge(phase_over, 4 * number)

        def load_weights(sp, k, c, src, kt=KT):
            if not (isinstance(c, int) and c == 0):
                sp.wait_ge(w_lo[k], c)
            sp.dma_start(w_raw[k][:, 0:kt, :], src).then_inc(raw_full[k], 16)

        def split_hi(act, k, c, kt=KT):
            act.wait_ge(raw_full[k], 16 * c + 16)
            if not (isinstance(c, int) and c == 0):
                act.wait_ge(gemm_over[k], c)
            nc.scalar.activation(W[k][0][:, 0:kt, :], w_raw[k][:, 0:kt, :], ACT.Copy).then_inc(w_hi[k], 1)

        def split_lo(dve, k, c, kt=KT):
            dve.wait_ge(w_hi[k], c + 1)
            nc.vector.tensor_tensor(W[k][1][:, 0:kt, :], w_raw[k][:, 0:kt, :],
                                    W[k][0][:, 0:kt, :].bitcast(F32), ALU.subtract).then_inc(w_lo[k], 1)

        def product(pe, k, c, moving, kt=KT, width=TB, blocks=3, ready=None):
            pe.wait_ge(w_lo[k], c + 1)
            if not (isinstance(c, int) and c == 0):
                pe.wait_ge(evacuated[k], c)
            for t in range(kt):
                if ready is not None:
                    pe.wait_ge(ready[0], ready[1] + t + 1)
                for n, (a, b) in enumerate(COMBOS):
                    for j in range(blocks):
                        last = nc.tensor.matmul(ps[:, 3 * k + j, 0:width], W[k][a][:, t, :],
                                                moving[b][:, t, j * width:(j + 1) * width],
                                                start=(t == 0 and n == 0), stop=(t == kt - 1 and n == 2))
            last.then_inc(gemm_over[k], 1)

        def norm_sems(tag):
            return {n: [sem(f"{tag}_{n}{k}") for k in range(2)]
                    for n in ("x_in", "squared", "rooted", "recip", "scaled", "turned", "hi")}

        def norm_load(sp, b, s, k, n, src):
            sp.wait_ge(s["scaled"][k], n)
            sp.dma_start(b["x_in"][k][:], src).then_inc(s["x_in"][k], 16)

        def norm_stats(act, b, s, k, n):
            act.wait_ge(s["x_in"][k], 16 * n + 16)
            nc.scalar.activation(b["junk"][:], b["x_in"][k][:], ACT.Square, accum_out=SUM[k]).then_inc(s["squared"][k], 1)
            act.wait_ge(s["squared"][k], n + 1)
            nc.scalar.activation(RC[k], SUM[k], ACT.Sqrt, bias=eps_t[:], scale=1.0 / D).then_inc(s["rooted"][k], 1)

        def norm_scale(dve, b, s, k, n):
            dve.wait_ge(s["rooted"][k], n + 1)
            nc.vector.reciprocal(NM[k], RC[k]).then_inc(s["recip"][k], 1)
            dve.wait_ge(s["recip"][k], n + 1)
            nc.vector.scalar_tensor_tensor(out=b["xs"][k][:], in0=b["x_in"][k][:], scalar=NM[k], in1=b["g"][:],
                                           op0=ALU.mult, op1=ALU.mult).then_inc(s["scaled"][k], 1)

        def norm_turn(pe, b, s, k, n, done):
            pe.wait_ge(s["scaled"][k], n + 1)
            pe.wait_ge(done[k], n)
            for t in range(KT):
                last = nc.tensor.transpose(ps[:, 2 * k + t // 4, (t % 4) * P:(t % 4 + 1) * P],
                                           b["xs"][k][:, t * P:(t + 1) * P], ident[:])
            last.then_inc(s["turned"][k], 1)

        def two_banks(k):
            return ps[:, 2 * k:2 * k + 2, :].rearrange("p a (b c) -> p (a b) c", c=P)

        def norm_hi(act, s, k, n, dst, tok):
            act.wait_ge(s["turned"][k], n + 1)
            nc.scalar.activation(dst[0][:, :, tok], two_banks(k), ACT.Copy).then_inc(s["hi"][k], 1)

        def norm_lo(dve, s, k, n, dst, tok, done):
            dve.wait_ge(s["hi"][k], n + 1)
            nc.vector.tensor_tensor(dst[1][:, :, tok], two_banks(k), dst[0][:, :, tok].bitcast(F32),
                                    ALU.subtract).then_inc(done[k], 1)

        xn_sems = norm_sems("xn")
        xn_done = [sem(f"xn_done{k}") for k in range(2)]

        def mem_use(t):
            return (NT + 1 - t % 2) // 2 + t // 2

        g_in = group("g", "attn", "mem", "mlp", "fin")

        def tile_rows(t):
            return ds(t * P, P)

        at_sems = group("at", "q_hi", "k_hi", "v_hi", "v_lo", "turned", "tokened", "stored", "saved", "negc_in",
                        "s_over", "s_read", "max", "negmax", "exp", "recip", "p_ready", "t_over", "pt_hi", "pt_lo",
                        "pv_over", "o_hi", "o_lo")

        class Shape:

            def __init__(self, buf, base, kv, kv_tiles, heads, causal, scale, q_scale, first=None):
                self.b, self.s, self.base, self.kv, self.kv_tiles = buf, at_sems, base, kv, kv_tiles
                self.heads, self.causal, self.scale, self.q_scale = heads, causal, scale, q_scale
                self.rows = P // heads
                self.units = [(h, i, (i + 1 if causal else kv_tiles)) for h in range(heads) for i in range(QT)]
                self.groups, n = [], 0
                for _, _, blocks in self.units:
                    g = [(n + x, 4 * x, min(blocks, 4 * x + 4)) for x in range((blocks + 3) // 4)]
                    n += len(g)
                    self.groups.append(g)
                self.n_groups = n
                self.per = len(self.units)
                self.width = kv_tiles * P // 3 if kv_tiles > 3 else kv_tiles * P
                self.blocks = 3 if kv_tiles > 3 else 1
                self.before = {n: 0 if first is None else first.total(n) for n in at_sems}

            def total(self, name):
                of = dict(turned=2, tokened=2, stored=64, negc_in=16, max=0, t_over=self.n_groups, pt_hi=self.n_groups,
                          pt_lo=self.n_groups, pv_over=self.per // 2, o_hi=self.per // 2, o_lo=self.per // 2,
                          q_hi=1, k_hi=1, v_hi=1, v_lo=1, saved=1)
                return BT * of.get(name, self.per)

            def kv_set(self, k):
                return ps[:, 3 * k:3 * k + self.blocks, 0:self.width]

        fox = Shape(fx, uses["fox"], A, NT, 2, True, 1.0, FD ** -0.5)
        mem = Shape(mx, uses["mem"], ME, MT, 1, False, MD ** -0.5, 1.0, fox)

        def blocked(ap, n):
            return ap.rearrange("p (j t) -> p j t", j=n)

        def attend_pe(pe, a, it):
            b, s = a.b, a.s
            c0, c1 = a.base[0] + 2 * it, a.base[1] + it
            product(pe, 0, c0, A)
            product(pe, 1, c1, a.kv, width=a.width, blocks=a.blocks)
            product(pe, 0, c0 + 1, a.kv, width=a.width, blocks=a.blocks)
            for k, src, c in ((1, b["kf"], c1 + 1), (0, b["vf"], c0 + 2)):
                pe.wait_ge(evacuated[k], c)
                for t in range(a.kv_tiles):
                    last = nc.tensor.transpose(ps[:, 3 * k + t // 3, (t % 3) * P:(t % 3 + 1) * P],
                                               src[:, t * P:(t + 1) * P], ident[:])
                last.then_inc(s["turned"], 1)
            pe.wait_ge(s["tokened"], 2 * it + 2 + a.before["tokened"])

            def scores(u):
                h, i, blocks = a.units[u]
                if u >= 2:
                    pe.wait_ge(s["s_read"], a.per * it + u - 1 + a.before["s_read"])
                r = slice(a.rows * h, a.rows * (h + 1))
                for lo in range(0, blocks * P, 512):
                    hi = min(lo + 512, blocks * P)
                    bank = 2 * (u % 2) + lo // 512
                    diag = a.causal and hi == blocks * P
                    for n, (x, y) in enumerate(COMBOS):
                        last = nc.tensor.matmul(ps[:, bank, 0:hi - lo], b["q"][x][r, i * P:(i + 1) * P],
                                                b["k"][y][r, lo:hi], start=(n == 0), stop=(n == 2 and not diag))
                    if diag:
                        last = nc.tensor.matmul(ps[:, bank, hi - lo - P:hi - lo], ident_r[:], causal_r[:],
                                                start=False, stop=True)
                last.then_inc(s["s_over"], 1)

            def turn(u):
                pe.wait_ge(s["p_ready"], a.per * it + u + 1 + a.before["p_ready"])
                for g, b0, b1 in a.groups[u]:
                    if g >= 2:
                        pe.wait_ge(s["pt_lo"], a.n_groups * it + g - 1 + a.before["pt_lo"])
                    for x in range(b0, b1):
                        last = nc.tensor.transpose(ps[:, 4 + g % 2, (x - b0) * P:(x - b0 + 1) * P],
                                                   b["p"][u % 2][:, x * P:(x + 1) * P], ident[:])
                    last.then_inc(s["t_over"], 1)

            def values(u):
                h, i, blocks = a.units[u]
                j = u // 2
                if j == 0:
                    pe.wait_ge(s["v_lo"], it + 1 + a.before["v_lo"])
                pe.wait_ge(s["pt_lo"], a.n_groups * it + a.groups[u][-1][0] + 1 + a.before["pt_lo"])
                if j >= 2:
                    pe.wait_ge(s["o_lo"], a.per // 2 * it + j - 1 + a.before["o_lo"])
                for x in range(blocks):
                    lo = P if a.causal and x == blocks - 1 else 0
                    for n, (y, z) in enumerate(COMBOS):
                        last = nc.tensor.matmul(ps[:, 6 + j % 2, lo:2 * P], b["v"][y][:, x, :],
                                                b["pt"][z][:, x, lo:2 * P],
                                                start=(x == 0 and n == 0), stop=(x == blocks - 1 and n == 2))
                last.then_inc(s["pv_over"], 1)

            scores(0)
            scores(1)
            for u in range(a.per + 1):
                if u < a.per:
                    turn(u)
                if u + 2 < a.per:
                    scores(u + 2)
                if u % 2 == 0 and u:
                    values(u - 1)

        def attend_act(act, a, it, saves):
            b, s = a.b, a.s
            c0, c1 = a.base[0] + 2 * it, a.base[1] + it
            split_hi(act, 1, c1)
            act.wait_ge(gemm_over[0], c0 + 1)
            nc.scalar.activation(blocked(b["q"][0][:], 3), pset(0), ACT.Copy, scale=a.q_scale).then_inc(s["q_hi"], 1)
            split_hi(act, 0, c0 + 1)
            act.wait_ge(gemm_over[1], c1 + 1)
            nc.scalar.activation(blocked(b["kf"][:], a.blocks), a.kv_set(1), ACT.Copy)
            nc.scalar.activation(blocked(b["k"][0][:], a.blocks), a.kv_set(1), ACT.Copy).then_inc(s["k_hi"], 1)
            act.wait_ge(s["q_hi"], it + 1 + a.before["q_hi"])
            last = nc.scalar.activation(saves[0][0][:, it, :], b["q"][0][:, SEQ:T].bitcast(F32), ACT.Copy)
            if a.causal:
                act.wait_ge(s["k_hi"], it + 1 + a.before["k_hi"])
                last = nc.scalar.activation(saves[1][0][:, it, :], b["k"][0][:, SEQ:T].bitcast(F32), ACT.Copy)
            last.then_inc(s["saved"], 1)
            act.wait_ge(s["tokened"], 2 * it + 2 + a.before["tokened"])
            nc.scalar.activation(b["v"][0][:], b["vtok"][:], ACT.Copy).then_inc(s["v_hi"], 1)

            def exponent(u):
                h, i, blocks = a.units[u]
                n = blocks * P
                act.wait_ge(s["negmax"], a.per * it + u + 1 + a.before["negmax"])
                if a.causal:
                    nc.scalar.activation(b["p"][u % 2][:, 0:n], b["p"][u % 2][:, 0:n], ACT.Exp, bias=NM[u % 2],
                                         accum_out=SUM[u % 2]).then_inc(s["exp"], 1)
                else:
                    if u >= 2:
                        act.wait_ge(s["t_over"], a.n_groups * it + a.groups[u - 2][-1][0] + 1 + a.before["t_over"])
                    nc.scalar.activation(b["p"][u % 2][:, 0:n], ps[:, 2 * (u % 2), 0:n], ACT.Exp, bias=NM[u % 2],
                                         scale=a.scale, accum_out=SUM[u % 2]).then_inc(s["s_read"], 1)

            def normalise(u):
                n = a.units[u][2] * P
                act.wait_ge(s["recip"], a.per * it + u + 1 + a.before["recip"])
                nc.scalar.activation(b["p"][u % 2][:, 0:n], b["p"][u % 2][:, 0:n], ACT.Copy,
                                     scale=RC[u % 2]).then_inc(s["p_ready"], 1)

            def turned_hi(u):
                if u % 2 == 0 and u:
                    act.wait_ge(s["pv_over"], a.per // 2 * it + u // 2 + a.before["pv_over"])
                for g, b0, b1 in a.groups[u]:
                    act.wait_ge(s["t_over"], a.n_groups * it + g + 1 + a.before["t_over"])
                    nc.scalar.activation(b["pt"][0][:, b0:b1, (u % 2) * P:(u % 2 + 1) * P],
                                         ps[:, 4 + g % 2, 0:(b1 - b0) * P].rearrange("p (x q) -> p x q", q=P),
                                         ACT.Copy).then_inc(s["pt_hi"], 1)

            def output_hi(u):
                h, i, _ = a.units[u]
                j = u // 2
                act.wait_ge(s["pv_over"], a.per // 2 * it + j + 1 + a.before["pv_over"])
                r = slice(a.rows * h, a.rows * (h + 1))
                nc.scalar.activation(O[0][r, it, (i - 1) * P:(i + 1) * P], ps[r, 6 + j % 2, 0:2 * P],
                                     ACT.Copy).then_inc(s["o_hi"], 1)

            for u in range(a.per + 2):
                if u < a.per:
                    exponent(u)
                if 1 <= u <= a.per:
                    turned_hi(u - 1)
                if u < a.per:
                    normalise(u)
                if u >= 3 and u % 2:
                    output_hi(u - 2)
            split_hi(act, 0, c0 + 2)

        def attend_dve(dve, a, it, saves):
            b, s = a.b, a.s
            c0, c1 = a.base[0] + 2 * it, a.base[1] + it
            split_lo(dve, 1, c1)
            dve.wait_ge(s["q_hi"], it + 1 + a.before["q_hi"])
            nc.vector.scalar_tensor_tensor(out=blocked(b["q"][1][:], 3), in0=pset(0), scalar=a.q_scale,
                                           in1=blocked(b["q"][0][:].bitcast(F32), 3), op0=ALU.mult,
                                           op1=ALU.subtract).then_inc(evacuated[0], 1)
            split_lo(dve, 0, c0 + 1)
            dve.wait_ge(s["k_hi"], it + 1 + a.before["k_hi"])
            nc.vector.tensor_tensor(blocked(b["k"][1][:], a.blocks), a.kv_set(1),
                                    blocked(b["k"][0][:].bitcast(F32), a.blocks), ALU.subtract).then_inc(evacuated[1], 1)
            dve.wait_ge(evacuated[0], c0 + 1)
            nc.vector.tensor_copy(saves[0][1][:, it, :], b["q"][1][:, SEQ:T].bitcast(F32))
            if a.causal:
                dve.wait_ge(evacuated[1], c1 + 1)
                nc.vector.tensor_copy(saves[1][1][:, it, :], b["k"][1][:, SEQ:T].bitcast(F32))
            dve.wait_ge(gemm_over[0], c0 + 2)
            nc.vector.tensor_copy(blocked(b["vf"][:], a.blocks), a.kv_set(0)).then_inc(evacuated[0], 1)
            last_tiles = min(a.kv_tiles, 3)
            for k, dst, n in ((1, "ktok", 1), (0, "vtok", 2)):
                dve.wait_ge(s["turned"], 2 * it + n + a.before["turned"])
                dve.wait_ge(s["stored"], 16 * (4 if a.causal else 2) * it + a.before["stored"])
                nc.vector.tensor_copy(b[dst][:].rearrange("p (j t) c -> p j (t c)", j=a.blocks),
                                      ps[:, 3 * k:3 * k + a.blocks, 0:last_tiles * P]).then_inc(s["tokened"], 1)
            dve.wait_ge(s["v_hi"], it + 1 + a.before["v_hi"])
            nc.vector.tensor_tensor(b["v"][1][:], b["vtok"][:], b["v"][0][:].bitcast(F32),
                                    ALU.subtract).then_inc(s["v_lo"], 1)
            if a.causal:
                dve.wait_ge(s["negc_in"], 16 * it + 16 + a.before["negc_in"])

            def largest(u):
                h, i, blocks = a.units[u]
                n = blocks * P
                dve.wait_ge(s["s_over"], a.per * it + u + 1 + a.before["s_over"])
                if u >= 2:
                    dve.wait_ge(s["t_over"], a.n_groups * it + a.groups[u - 2][-1][0] + 1 + a.before["t_over"])
                logits = ps[:, 2 * (u % 2):2 * (u % 2) + 2, :].rearrange("p a c -> p (a c)")[:, 0:n]
                if a.causal:
                    nc.vector.memset(small[:, 15:16], 0.0)
                    nc.vector.tensor_tensor_reduce(out=b["p"][u % 2][:, 0:n], in0=logits, in1=b["negc"][:, h, 0:n],
                                                   scale=1.0, scalar=-3.0e38, op0=ALU.add, op1=ALU.max,
                                                   accum_out=MX[u % 2]).then_inc(s["s_read"], 1)
                    dve.wait_ge(s["s_read"], a.per * it + u + 1 + a.before["s_read"])
                else:
                    nc.vector.tensor_reduce(MX[u % 2], logits, AX_X, ALU.max).then_inc(s["max"], 1)
                    dve.wait_ge(s["max"], a.per * it + u + 1 + a.before["max"])
                nc.vector.tensor_scalar(NM[u % 2], MX[u % 2], -a.scale, None, ALU.mult).then_inc(s["negmax"], 1)

            def reciprocal(u):
                done = "exp" if a.causal else "s_read"
                dve.wait_ge(s[done], a.per * it + u + 1 + a.before[done])
                nc.vector.reciprocal(RC[u % 2], SUM[u % 2]).then_inc(s["recip"], 1)

            def turned_lo(u):
                for g, b0, b1 in a.groups[u]:
                    dve.wait_ge(s["pt_hi"], a.n_groups * it + g + 1 + a.before["pt_hi"])
                    cols = slice((u % 2) * P, (u % 2 + 1) * P)
                    nc.vector.tensor_tensor(b["pt"][1][:, b0:b1, cols],
                                            ps[:, 4 + g % 2, 0:(b1 - b0) * P].rearrange("p (x q) -> p x q", q=P),
                                            b["pt"][0][:, b0:b1, cols].bitcast(F32), ALU.subtract).then_inc(s["pt_lo"], 1)

            def output_lo(u):
                h, i, _ = a.units[u]
                j = u // 2
                dve.wait_ge(s["o_hi"], a.per // 2 * it + j + 1 + a.before["o_hi"])
                r = slice(a.rows * h, a.rows * (h + 1))
                cols = slice((i - 1) * P, (i + 1) * P)
                nc.vector.tensor_tensor(O[1][r, it, cols], ps[r, 6 + j % 2, 0:2 * P],
                                        O[0][r, it, cols].bitcast(F32), ALU.subtract).then_inc(s["o_lo"], 1)

            largest(0)
            for u in range(a.per + 2):
                if u + 1 < a.per:
                    largest(u + 1)
                if u < a.per:
                    reciprocal(u)
                if 1 <= u <= a.per:
                    turned_lo(u - 1)
                if u >= 3 and u % 2:
                    output_lo(u - 2)
            split_lo(dve, 0, c0 + 2)

        sample_sems = group("sample", "k_in", "v_in", "vn_in", "bias_in", "q_clear", "q_pad", "kt_over", "kt_hi",
                            "kt_lo", "s_over", "masked", "s_read", "negmax", "exp", "recip", "p_ready", "pt_over",
                            "pt_hi", "pt_lo", "v_hi", "v_lo", "pv_over", "om", "ot_over", "o_hi", "o_lo", "block",
                            "block_step")

        class Sample:
            def __init__(self, buf, new, tiles, heads, queries, cache_k, cache_v, scale):
                self.base = 0 if new else NB
                self.s = sample_sems
                self.b, self.new, self.tiles, self.heads, self.q = buf, new, tiles, heads, queries
                self.k_dram, self.v_dram, self.scale = cache_k, cache_v, scale
                self.per = heads // 4
                self.n = tiles * P + (NQ if new else 0)

        heads_flat = lambda c: c.rearrange("l b (t p) h d -> (l b) p t (h d)", p=P)
        sfox = Sample(sf, True, ST, FH, QS, heads_flat(cache_fox_k), heads_flat(cache_fox_v), 1.0)
        smem = Sample(sm, False, MT, MH, MQS, heads_flat(cache_mem_k), heads_flat(cache_mem_v), MD ** -0.5)

        def sample_block_mask(pool, a):
            ones = a.b["block"]
            nc.gpsimd.memset(ones[:], 1.0).then_inc(a.s["block_step"], 1)
            view = ones[:].rearrange("p (h d) -> p h d", h=a.heads)
            n = 2 * (a.base // NB)
            pool.wait_ge(a.s["block_step"], n + 1)
            nc.gpsimd.affine_select(out=view, in_=view, compare_op=ALU.is_ge, fill=0.0, base=0,
                                    pattern=[[-NQ, a.heads], [0, 512 // a.heads]],
                                    channel_multiplier=1).then_inc(a.s["block_step"], 1)
            pool.wait_ge(a.s["block_step"], n + 2)
            nc.gpsimd.affine_select(out=view, in_=view, compare_op=ALU.is_ge, fill=0.0, base=NQ - 1,
                                    pattern=[[NQ, a.heads], [0, 512 // a.heads]],
                                    channel_multiplier=-1).then_inc(a.s["block"], 1)


        def sample_loads(sp, a, i):
            b, s, c = a.b, a.s, i + a.base
            sp.wait_ge(s["kt_over"], c * 4)
            sp.dma_start(b["kraw"][:], a.k_dram[i]).then_inc(s["k_in"], 16)
            if a.new:
                sp.wait_ge(s["s_read"], c)
                sp.dma_start(b["bias"][:], negc_s[ds(i * (FH * NQ), FH * NQ), :]).then_inc(s["bias_in"], 16)
            sp.wait_ge(s["v_lo"], c)
            sp.dma_start(b["vraw"][:], a.v_dram[i]).then_inc(s["v_in"], 16)
            if a.new:
                sp.dma_start(b["vnraw"][:], vs_out[ds(i * NQ, NQ), :]).then_inc(s["vn_in"], 16)

        def sample_turn_keys(pe, a, i):
            b, s, c = a.b, a.s, i + a.base
            pe.wait_ge(s["k_in"], 16 * c + 16)
            for j in range(4):
                if j >= 2:
                    pe.wait_ge(s["kt_lo"], 4 * c + j - 1)
                for t in range(a.tiles):
                    last = nc.tensor.transpose(ps[:, j % 2, t * P:(t + 1) * P], b["kraw"][:, t, j * P:(j + 1) * P],
                                               ident[:])
                last.then_inc(s["kt_over"], 1)

        def sample_scores(pe, a, i):
            b, s, c = a.b, a.s, i + a.base
            pe.wait_ge(s["q_pad"], 2 * c + 2)
            for j in range(4):
                pe.wait_ge(s["kt_lo"], 4 * c + j + 1)
                for n, (x, y) in enumerate(COMBOS):
                    first, end = j == 0 and n == 0, j == 3 and n == 2
                    stat = b["qpad"][x][:, j * P:(j + 1) * P]
                    last = nc.tensor.matmul(ps[:, 2, 0:a.tiles * P], stat, b["kt"][y][:, j, :], start=first, stop=end)
                    if a.new:
                        last = nc.tensor.matmul(ps[:, 3, 0:NQ], stat, KS[y][:, j, ds(i * NQ, NQ)],
                                                start=first, stop=end)
            last.then_inc(s["s_over"], 1)

        def sample_turn(pe, a, i):
            b, s, c = a.b, a.s, i + a.base
            pe.wait_ge(s["p_ready"], c + 1)
            for t in range(a.tiles):
                last = nc.tensor.transpose(ps[:, 4, t * P:(t + 1) * P], b["p"][:, t * P:(t + 1) * P], ident[:])
            if a.new:
                last = nc.tensor.transpose(ps[0:NQ, 5, 0:P], b["p"][:, a.tiles * P:a.n], ident[:])
            last.then_inc(s["pt_over"], 1)

        def sample_values(pe, a, i):
            b, s, c = a.b, a.s, i + a.base
            pe.wait_ge(s["pt_lo"], c + 1)
            pe.wait_ge(s["v_lo"], c + 1)
            pe.wait_ge(s["om"], c)
            for n, (x, y) in enumerate(COMBOS):
                for t in range(a.tiles):
                    end = n == 2 and t == a.tiles - 1 and not a.new
                    last = nc.tensor.matmul(ps[:, 6, :], b["pt"][x][:, t, :], b["v"][y][:, t, :],
                                            start=(n == 0 and t == 0), stop=end)
                if a.new:
                    last = nc.tensor.matmul(ps[:, 6, :], b["pt"][x][0:NQ, a.tiles, :], b["vn"][y][:],
                                            start=False, stop=(n == 2))
            last.then_inc(s["pv_over"], 1)
            pe.wait_ge(s["om"], c + 1)
            pe.wait_ge(s["o_lo"], c)
            for j in range(4):
                last = nc.tensor.matmul(ps[:, 7, j * NQ:(j + 1) * NQ], b["om"][:, j * P:(j + 1) * P], rsel[:],
                                        start=True, stop=True)
            last.then_inc(s["ot_over"], 1)

        def sample_hi_keys(act, a, i):
            b, s, c = a.b, a.s, i + a.base
            act.wait_ge(s["s_over"], c)
            for j in range(4):
                act.wait_ge(s["kt_over"], 4 * c + j + 1)
                nc.scalar.activation(b["kt"][0][:, j, :], ps[:, j % 2, 0:a.tiles * P], ACT.Copy).then_inc(s["kt_hi"], 1)

        def sample_lo_keys(dve, a, i):
            b, s, c = a.b, a.s, i + a.base
            for j in range(4):
                dve.wait_ge(s["kt_hi"], 4 * c + j + 1)
                nc.vector.tensor_tensor(b["kt"][1][:, j, :], ps[:, j % 2, 0:a.tiles * P],
                                        b["kt"][0][:, j, :].bitcast(F32), ALU.subtract).then_inc(s["kt_lo"], 1)

        def sample_pad(dve, a, i):
            b, s, c = a.b, a.s, i + a.base
            dve.wait_ge(s["s_over"], c)
            for x in range(2):
                w = P + NQ * a.per
                for h in range(a.per):
                    r = slice(P // a.per * h, P // a.per * (h + 1))
                    dst = b["qpad"][x][r, :].rearrange("p (j w) -> p j w", w=w)[:, :, h * NQ:(h + 1) * NQ]
                    last = nc.vector.tensor_copy(dst, a.q[x][r, :, ds(i * NQ, NQ)].bitcast(F32))
                last.then_inc(s["q_pad"], 1)

        def sample_pe(pe, a, i, more):
            sample_scores(pe, a, i)
            if more:
                sample_turn_keys(pe, a, i + 1)
            sample_turn(pe, a, i)
            sample_values(pe, a, i)

        def sample_act(act, a, i, more):
            b, s, c = a.b, a.s, i + a.base
            act.wait_ge(s["negmax"], c + 1)
            src = b["p"][:, 0:a.n] if a.new else ps[:, 2, 0:a.n]
            nc.scalar.activation(b["p"][:, 0:a.n], src, ACT.Exp, bias=NM[0], scale=a.scale,
                                 accum_out=SUM[0]).then_inc(s["exp"], 1)
            act.wait_ge(s["recip"], c + 1)
            nc.scalar.activation(b["p"][:, 0:a.n], b["p"][:, 0:a.n], ACT.Copy, scale=RC[0]).then_inc(s["p_ready"], 1)
            act.wait_ge(s["pv_over"], c)
            act.wait_ge(s["v_in"], 16 * c + 16)
            last = nc.scalar.activation(b["v"][0][:], b["vraw"][:], ACT.Copy)
            if a.new:
                act.wait_ge(s["vn_in"], 16 * c + 16)
                last = nc.scalar.activation(b["vn"][0][:], b["vnraw"][:], ACT.Copy)
            last.then_inc(s["v_hi"], 1)
            if more:
                sample_hi_keys(act, a, i + 1)
            act.wait_ge(s["pt_over"], c + 1)
            last = nc.scalar.activation(b["pt"][0][:, 0:a.tiles, :],
                                        ps[:, 4, 0:a.tiles * P].rearrange("p (t q) -> p t q", q=P), ACT.Copy)
            if a.new:
                last = nc.scalar.activation(b["pt"][0][0:NQ, a.tiles, :], ps[0:NQ, 5, 0:P], ACT.Copy)
            last.then_inc(s["pt_hi"], 1)
            act.wait_ge(s["ot_over"], c + 1)
            nc.scalar.activation(O[0][:, :, ds(SEQ + i * NQ, NQ)],
                                 ps[:, 7, 0:4 * NQ].rearrange("p (j q) -> p j q", q=NQ), ACT.Copy).then_inc(s["o_hi"], 1)

        def sample_dve(dve, a, i, more):
            b, s, c = a.b, a.s, i + a.base
            if a.new:
                dve.wait_ge(s["bias_in"], 16 * c + 16)
                new = b["bias"][:, a.tiles * P:a.n]
                nc.vector.tensor_tensor(new, new, mask_new[:], ALU.add).then_inc(s["masked"], 1)
                dve.wait_ge(s["masked"], c + 1)
                dve.wait_ge(s["s_over"], c + 1)
                dve.wait_ge(s["pt_over"], c)
                logits = ps[:, 2:4, :].rearrange("p a c -> p (a c)")[:, 0:a.n]
                nc.vector.memset(small[:, 15:16], 0.0)
                nc.vector.tensor_tensor_reduce(out=b["p"][:, 0:a.n], in0=logits, in1=b["bias"][:], scale=1.0,
                                               scalar=-3.0e38, op0=ALU.add, op1=ALU.max,
                                               accum_out=MX[0]).then_inc(s["s_read"], 1)
                dve.wait_ge(s["s_read"], c + 1)
            else:
                dve.wait_ge(s["s_over"], c + 1)
                nc.vector.tensor_reduce(MX[0], ps[:, 2, 0:a.n], AX_X, ALU.max).then_inc(s["s_read"], 1)
                dve.wait_ge(s["s_read"], c + 1)
            nc.vector.tensor_scalar(NM[0], MX[0], -a.scale, None, ALU.mult).then_inc(s["negmax"], 1)
            dve.wait_ge(s["exp"], c + 1)
            nc.vector.reciprocal(RC[0], SUM[0]).then_inc(s["recip"], 1)
            dve.wait_ge(s["v_hi"], c + 1)
            last = nc.vector.tensor_tensor(b["v"][1][:], b["vraw"][:], b["v"][0][:].bitcast(F32), ALU.subtract)
            if a.new:
                last = nc.vector.tensor_tensor(b["vn"][1][:], b["vnraw"][:], b["vn"][0][:].bitcast(F32), ALU.subtract)
            last.then_inc(s["v_lo"], 1)
            if more:
                sample_lo_keys(dve, a, i + 1)
                sample_pad(dve, a, i + 1)
            dve.wait_ge(s["pt_hi"], c + 1)
            last = nc.vector.tensor_tensor(b["pt"][1][:, 0:a.tiles, :],
                                           ps[:, 4, 0:a.tiles * P].rearrange("p (t q) -> p t q", q=P),
                                           b["pt"][0][:, 0:a.tiles, :].bitcast(F32), ALU.subtract)
            if a.new:
                last = nc.vector.tensor_tensor(b["pt"][1][0:NQ, a.tiles, :], ps[0:NQ, 5, 0:P],
                                               b["pt"][0][0:NQ, a.tiles, :].bitcast(F32), ALU.subtract)
            last.then_inc(s["pt_lo"], 1)
            dve.wait_ge(s["pv_over"], c + 1)
            nc.vector.tensor_tensor(b["om"][:], ps[:, 6, :], b["block"][:], ALU.mult).then_inc(s["om"], 1)
            dve.wait_ge(s["o_hi"], c + 1)
            cols = ds(SEQ + i * NQ, NQ)
            nc.vector.tensor_tensor(O[1][:, :, cols], ps[:, 7, 0:4 * NQ].rearrange("p (j q) -> p j q", q=NQ),
                                    O[0][:, :, cols].bitcast(F32), ALU.subtract).then_inc(s["o_lo"], 1)

        def gate_weights(r, n):
            return win[:, :, ds(n * P + (C_G + r * D), P)]

        def merge_sp(sp, r, after):
            c0, c1 = uses[f"merge{r}"]
            with sp.Fori(0, KT - 1) as n:
                load_weights(sp, 1, n + c1, wbr[r][:, :, ds(n * P, P)], BT)
                load_weights(sp, 0, n + (c0 + 1), gate_weights(r, n + 1))
            load_weights(sp, 1, c1 + KT - 1, wbr[r][:, :, D - P:D], BT)
            load_weights(sp, 0, c0 + KT, after)

        def merge_pe(pe, r):
            c0, c1 = uses[f"merge{r}"]
            with pe.Fori(0, KT) as n:
                product(pe, 0, n + c0, A)
                product(pe, 1, n + c1, O, kt=BT)

        def merge_act(act, r):
            c0, c1 = uses[f"merge{r}"]
            with act.Fori(0, KT) as n:
                split_hi(act, 1, n + c1, BT)
                act.wait_ge(gemm_over[0], n + (c0 + 1))
                act.wait_ge(evacuated[1], n + c1)
                nc.scalar.activation(blocked(mg["gate"][:], 3), pset(0), ACT.Sigmoid).then_inc(evacuated[0], 1)
                split_hi(act, 0, n + (c0 + 1))

        def merge_dve(dve, r):
            c0, c1 = uses[f"merge{r}"]
            with dve.Fori(0, KT) as n:
                split_lo(dve, 1, n + c1, BT)
                dve.wait_ge(evacuated[0], n + (c0 + 1))
                dve.wait_ge(gemm_over[1], n + (c1 + 1))
                dst = H[:, n, :] if r == 0 else mg["prod"][:]
                nc.vector.tensor_tensor(blocked(dst, 3), pset(1), blocked(mg["gate"][:], 3),
                                        ALU.mult).then_inc(evacuated[1], 1)
                if r:
                    dve.wait_ge(evacuated[1], n + (c1 + 1))
                    nc.vector.tensor_tensor(H[:, n, :], H[:, n, :], mg["prod"][:], ALU.add)
                split_lo(dve, 0, n + (c0 + 1))

        fs = group("forget", "neg", "exp", "plus", "ln", "logf", "neg_logf", "turned", "tok", "cache_in", "new_in",
                   "cache_turned", "ext", "c", "cs", "c_stored", "stored", "b_in", "zero", "masks", "mask_sum")
        po = group("pool", "hist_in", "w_in", "w_hi", "w_lo", "hist_t", "clear", "hist", "u", "tail_t", "tail", "step",
                   "first", "pooled", "d_hi", "d_lo", "mix_over", "o_hi", "o_lo", "stored")
        ou = group("out", "m_hi", "m_lo", "turned0", "turned1", "xtok_in0", "xtok_in1", "xt", "sq", "acc", "ones",
                   "summed", "rooted", "rstd", "hn", "n_hi", "n_lo")
        ff = group("ffn", "a", "hi", "lo")
        fin = {n: [sem(f"fin_{n}{k}") for k in range(2)] for n in ("turned", "squared", "rooted", "recip", "y", "stored")}
        NLOOP = QT // 2
        HALF = (CH + KT) // 2
        U0, U1 = uses["ffn"]

        def ffn_use(it, j):
            return it * HALF + (uses["ffn"][j % 2] + j // 2)

        block = ctx.enter_context(nc.Block())

        @block.sync
        def _(sp):
            sp.dma_start(bn["g"][:], g_attn.rearrange("l d -> (l d)").partition_broadcast(P)).then_inc(g_in["attn"], 16)
            with sp.Fori(0, NLOOP) as it:
                for k in range(2):
                    norm_load(sp, bn, xn_sems, k, it, xp_rows[:, 2 * it + k, :])
            norm_load(sp, bn, xn_sems, 0, NLOOP, xs_rows)
            load_weights(sp, 1, 0, win[:, :, C_F:C_F + P])
            load_weights(sp, 0, 0, win[:, :, 0:P])
            sp.dma_start(s_col[:], s_pool.rearrange("l (g p) -> p (l g)", p=P),
                         allow_slow_non_contiguous=True).then_inc(consts_in, 16)
            sp.dma_start(g_col[:], g_mlp.rearrange("l (g p) -> p (l g)", p=P),
                         allow_slow_non_contiguous=True).then_inc(consts_in, 16)
            next_phase(sp, 1)
            sp.dma_start(bf["bf"][:], b_f.rearrange("l h -> h l"), allow_slow_non_contiguous=True).then_inc(fs["b_in"], 16)
            for t in range(ST):
                sp.dma_start(bf["cache"][:, t, :].rearrange("p (b h) -> p b h", b=NB),
                             cache_fox_logf.rearrange("l b (t p) h -> t p (l b) h", p=P)[t]).then_inc(fs["cache_in"], 16)
            sp.wait_ge(fs["neg_logf"], 1)
            for i in range(NB):
                sp.dma_start(bf["ext"][i * FH:(i + 1) * FH, PAST:PAST + NQ],
                             bf["nl"][:, SEQ + i * NQ:SEQ + (i + 1) * NQ]).then_inc(fs["new_in"], 16)
            sp.wait_ge(fs["tok"], 1)
            sp.dma_start(new_fox_logf_p.rearrange("l a (t p) h -> p (l a t) h", p=P),
                         bf["tok"][:, 0:QT, :]).then_inc(fs["stored"], 16)
            sp.dma_start(new_fox_logf_s.rearrange("l b q h -> (l b q) h"), bf["tok"][:, QT, :]).then_inc(fs["stored"], 16)
            sp.wait_ge(fs["c"], 1)
            sp.dma_start(negc_p.rearrange("a (b s) -> (a b) s", b=2), bf["c"][:]).then_inc(fs["c_stored"], 16)
            sp.wait_ge(fs["cs"], 1)
            sp.dma_start(negc_s.rearrange("(r q) c -> r q c", q=NQ),
                         bf["cs"][:].unsqueeze(1).broadcast_to([NB * FH, NQ, PAST + NQ])).then_inc(fs["c_stored"], 16)
            sp.wait_ge(fs["c_stored"], 32)
            sp.wait_ge(fs["stored"], 32)
            next_phase(sp, 2)

            def attend_sp(a, it, w_k, w_v, after):
                b, s = a.b, a.s
                c0, c1 = it * 2 + a.base[0], it + a.base[1]
                load_weights(sp, 1, c1, w_k)
                if a.causal:
                    sp.wait_ge(s["s_read"], it * a.per + a.before["s_read"])
                load_weights(sp, 0, c0 + 1, w_v)
                if a.causal:
                    sp.dma_start(b["negc"][:].rearrange("p h s -> p (h s)"),
                                 negc_p[it].partition_broadcast(P)).then_inc(s["negc_in"], 16)
                load_weights(sp, 0, c0 + 2, after)
                for n, buf, big, rest in ((1, "ktok", kp_out if a.causal else mk_out, ks_out),
                                          (2, "vtok", vp_out if a.causal else mv_out, vs_out)):
                    sp.wait_ge(s["tokened"], it * 2 + n + a.before["tokened"])
                    if n == 1:
                        sp.sem_inc(sp_passed, 1)
                    tiles = QT if a.causal else MT
                    sp.dma_start(big[:, :, ds(it * P, P)], b[buf][:, 0:tiles, :]).then_inc(s["stored"], 16)
                    if a.causal:
                        sp.dma_start(rest[:, ds(it * P, P)], b[buf][:, QT, :]).then_inc(s["stored"], 16)

            def fox_k_v(it):
                return win[:, :, ds(it * P + FW, P)], win[:, :, ds(it * P + 2 * FW, P)]

            def mem_k_v(it):
                return wmkv[:, :, ds(it * P, P)], wmkv[:, :, ds(it * P + MH * MD, P)]

            with sp.Fori(0, BT - 1) as it:
                attend_sp(fox, it, *fox_k_v(it), win[:, :, ds(it * P + P, P)])
            attend_sp(fox, BT - 1, *fox_k_v(BT - 1), gate_weights(0, 0))
            sp.wait_ge(fox.s["stored"], 64 * BT)
            next_phase(sp, 3)
            with sp.Fori(0, NB) as i:
                sample_loads(sp, sfox, i)
            next_phase(sp, 4, wait=False)
            merge_sp(sp, 0, win[:, :, C_U:C_U + P])
            next_phase(sp, 5)
            sp.dma_start(pb["hist"][:], cache_pool.rearrange("l b j c -> (l b j) c")).then_inc(po["hist_in"], 16)
            sp.dma_start(pb["wraw"][:], w_pool.rearrange("l g c d -> c (l g) d")).then_inc(po["w_in"], 16)
            for g in range(1, BT):
                load_weights(sp, g % 2, uses["pool"][g % 2] + g // 2, win[:, :, C_U + g * P:C_U + (g + 1) * P])
            load_weights(sp, 0, uses["merge1"][0], gate_weights(1, 0))
            sp.wait_ge(po["tail"], BT)
            sp.dma_start(new_pool_p.rearrange("l a j c -> (l a j) c"), pb["tail"][P - HIST:P, 0, :]).then_inc(po["stored"], 16)
            for i in range(NB):
                sp.dma_start(new_pool_s.rearrange("l b j c -> (l b) j c")[i],
                             pb["tail"][(i + 1) * NQ - HIST:(i + 1) * NQ, 1, :]).then_inc(po["stored"], 16)
            sp.wait_ge(po["stored"], 16 * (1 + NB))
            next_phase(sp, 6, wait=False)
            merge_sp(sp, 1, win[:, :, C_QM:C_QM + P])
            next_phase(sp, 7)
            sp.dma_start(bm["g"][:], g_mem.rearrange("l d -> (l d)").partition_broadcast(P)).then_inc(g_in["mem"], 16)
            for t in range(MT):
                norm_load(sp, bm, xn_sems, t % 2, mem_use(t), mem_rows[:, t, :])
            next_phase(sp, 8, wait=False)
            with sp.Fori(0, BT - 1) as it:
                attend_sp(mem, it, *mem_k_v(it), win[:, :, ds(it * P + (C_QM + P), P)])
            attend_sp(mem, BT - 1, *mem_k_v(BT - 1), gate_weights(2, 0))
            sp.wait_ge(mem.s["stored"], (64 + 32) * BT)
            next_phase(sp, 9)
            with sp.Fori(0, NB) as i:
                sample_loads(sp, smem, i)
            next_phase(sp, 10, wait=False)
            merge_sp(sp, 2, wout[:, :, 0:P])
            next_phase(sp, 11)

            def out_sp(it, after):
                for k in range(2):
                    sp.wait_ge(ou[f"turned{k}"], it * 2)
                    cols = ds(it * (2 * P) + k * P, P)
                    sp.dma_start(ob["xtok"][k][:, 0:QT, :], xp_rows[:, :, cols]).then_inc(ou[f"xtok_in{k}"], 16)
                    sp.dma_start(ob["xtok"][k][:, QT, :], xs_rows[:, cols]).then_inc(ou[f"xtok_in{k}"], 16)
                    if k == 0:
                        load_weights(sp, 1, it + uses["out"][1], wout[:, :, ds(it * (2 * P) + P, P)])
                load_weights(sp, 0, it + (uses["out"][0] + 1), after)

            with sp.Fori(0, KT // 2 - 1) as it:
                out_sp(it, wout[:, :, ds(it * (2 * P) + 2 * P, P)])
            out_sp(KT // 2 - 1, wup[:, :, 0:P])

            def ffn_sp(it, after):
                for j in range(1, CH):
                    load_weights(sp, j % 2, ffn_use(it, j), wup[:, :, ds(it * (CH * P) + j * P, P)])
                for j in range(KT):
                    load_weights(sp, j % 2, ffn_use(it, CH + j), wdown[:, ds(it * CH, CH), j * P:(j + 1) * P], CH)
                if after is not None:
                    load_weights(sp, 0, ffn_use(it + 1, 0), after)

            with sp.Fori(0, NCH - 1) as it:
                ffn_sp(it, wup[:, :, ds(it * (CH * P) + CH * P, P)])
            ffn_sp(NCH - 1, None)
            next_phase(sp, 12)
            sp.dma_start(yb["g"][:], g_final.partition_broadcast(P)).then_inc(g_in["fin"], 16)
            yp_rows = y_prompt.rearrange("a (t p) d -> p (a t) d", p=P)
            for t in range(NT):
                k = t % 2
                sp.wait_ge(fin["y"][k], t // 2 + 1)
                dst = yp_rows[:, t, :] if t < QT else y_sample.rearrange("b q d -> (b q) d")
                sp.dma_start(dst, yb["y"][k][:]).then_inc(fin["stored"][k], 16)
            sp.wait_ge(fin["stored"][0], 16 * ((NT + 1) // 2))
            sp.wait_ge(fin["stored"][1], 16 * (NT // 2))

        @block.gpsimd
        def _(pool):
            step = [0]

            def then_next(ins):
                step[0] += 1
                ins.then_inc(consts_step, 1)
                pool.wait_ge(consts_step, step[0])

            nc.gpsimd.memset(eps_t[:], EPS)
            for t in range(16):
                nc.gpsimd.memset(cnt_col[:, t:t + 1], 1.0 / (t + 1))
            then_next(nc.gpsimd.memset(ident[:], 0.0))
            nc.gpsimd.affine_select(out=ident[:], in_=ident[:], compare_op=ALU.not_equal, fill=1.0, base=0,
                                    pattern=[[-1, P]], channel_multiplier=1).then_inc(consts_made, 1)
            pool.wait_ge(phase_over, 4)
            nc.gpsimd.memset(bf["m3"][:], 1.0)
            nc.gpsimd.memset(bf["m4"][:], 1.0)
            then_next(nc.gpsimd.memset(bf["cm"][:], 0.0))
            nc.gpsimd.affine_select(out=bf["cm"][:], in_=bf["cm"][:], compare_op=ALU.is_ge, fill=-BIG, base=0,
                                    pattern=[[-1, P]], channel_multiplier=1)
            nc.gpsimd.affine_select(out=bf["m3"][:], in_=bf["m3"][:], compare_op=ALU.is_equal, fill=0.0, base=0,
                                    pattern=[[-NQ, NB], [-1, NQ]], channel_multiplier=1)
            then_next(nc.gpsimd.affine_select(out=bf["m4"][:], in_=bf["m4"][:], compare_op=ALU.is_ge, fill=0.0,
                                              base=0, pattern=[[-NQ, NB], [-1, NQ]], channel_multiplier=1))
            nc.gpsimd.affine_select(out=bf["m4"][:], in_=bf["m4"][:], compare_op=ALU.is_ge, fill=0.0, base=NQ - 1,
                                    pattern=[[NQ, NB], [0, NQ]], channel_multiplier=-1).then_inc(fs["masks"], 1)
            pool.wait_ge(phase_over, 12)
            sample_block_mask(pool, sfox)
            pool.wait_ge(phase_over, 36)
            sample_block_mask(pool, smem)

        @block.tensor
        def _(pe):
            pe.wait_ge(consts_made, 1)
            with pe.Fori(0, NLOOP) as it:
                for k in range(2):
                    norm_turn(pe, bn, xn_sems, k, it, xn_done)
            norm_turn(pe, bn, xn_sems, 0, NLOOP, xn_done)
            next_phase(pe, 1)
            product(pe, 1, 0, A)
            pe.wait_ge(fs["logf"], 1)
            for t in range(NT):
                last = nc.tensor.transpose(ps[:, 0, t * FH:(t + 1) * FH], bf["x"][:, t * P:(t + 1) * P],
                                           ident[0:FH, 0:FH])
            last.then_inc(fs["turned"], 1)
            pe.wait_ge(fs["cache_in"], 16 * ST)
            for t in range(ST):
                last = nc.tensor.transpose(ps[0:NB * FH, 1, t * P:(t + 1) * P], bf["cache"][:, t, :], ident[:])
            last.then_inc(fs["cache_turned"], 1)
            next_phase(pe, 2)
            with pe.Fori(0, BT) as it:
                attend_pe(pe, fox, it)
            next_phase(pe, 3)
            sample_turn_keys(pe, sfox, 0)
            with pe.Fori(0, NB - 1) as i:
                sample_pe(pe, sfox, i, True)
            sample_pe(pe, sfox, NB - 1, False)
            next_phase(pe, 4)
            merge_pe(pe, 0)
            next_phase(pe, 5)
            pe.wait_ge(po["hist_in"], 16)
            for g in range(BT):
                last = nc.tensor.transpose(ps[:, 6, g * P:g * P + NB * HIST], pb["hist"][:, g * P:(g + 1) * P],
                                           ident[0:NB * HIST, 0:NB * HIST])
            last.then_inc(po["hist_t"], 1)
            for g in range(BT + 1):
                if g < BT:
                    product(pe, g % 2, uses["pool"][g % 2] + g // 2, A)
                if g >= 1:
                    pe.wait_ge(po["u"], g)
                    if g >= 2:
                        pe.wait_ge(po["tail"], g - 1)
                    for x in range(2):
                        last = nc.tensor.transpose(ps[:, 7, x * P:(x + 1) * P], pb["uf"][:, x * P:(x + 1) * P], ident[:])
                    last.then_inc(po["tail_t"], 1)
            pe.wait_ge(po["w_lo"], 1)
            for k in range(2):
                pe.wait_ge(evacuated[k], uses["merge1"][k])
            for g in range(BT):
                pe.wait_ge(po["d_lo"], g + 1)
                if g >= 2:
                    pe.wait_ge(po["o_lo"], g - 1)
                for n, (x, y) in enumerate(COMBOS):
                    for j in range(3):
                        last = nc.tensor.matmul(ps[:, 3 * (g % 2) + j, 0:TB], pb["w"][x][:, g, :],
                                                O[y][:, g, j * TB:(j + 1) * TB], start=(n == 0), stop=(n == 2))
                last.then_inc(po["mix_over"], 1)
            next_phase(pe, 6)
            merge_pe(pe, 1)
            next_phase(pe, 7)
            for t in range(MT):
                norm_turn(pe, bm, xn_sems, t % 2, mem_use(t), xn_done)
            next_phase(pe, 8)
            with pe.Fori(0, BT) as it:
                attend_pe(pe, mem, it)
            next_phase(pe, 9)
            sample_turn_keys(pe, smem, 0)
            with pe.Fori(0, NB - 1) as i:
                sample_pe(pe, smem, i, True)
            sample_pe(pe, smem, NB - 1, False)
            next_phase(pe, 10)
            merge_pe(pe, 2)
            next_phase(pe, 11)
            with pe.Fori(0, KT // 2) as it:
                for k in range(2):
                    pe.wait_ge(ou[f"xtok_in{k}"], it * 32 + 32)
                    pe.wait_ge(ou["xt"], it * 4 + 2 * k)
                    for t in range(QT):
                        last = nc.tensor.transpose(ps[:, 6 + t // 4, (t % 4) * P:(t % 4 + 1) * P],
                                                   ob["xtok"][k][:, t, :], ident[:])
                    last.then_inc(ou[f"turned{k}"], 1)
                    product(pe, k, it + uses["out"][k], A, ready=(ou["m_lo"], 0))
                    pe.wait_ge(ou["xt"], it * 4 + (2 * k + 1))
                    nc.tensor.transpose(ps[:, 6, 0:P], ob["xtok"][k][:, QT, :], ident[:]).then_inc(ou[f"turned{k}"], 1)
            pe.wait_ge(ou["ones"], 1)
            pe.wait_ge(ou["acc"], KT)
            pe.wait_ge(evacuated[0], U0)
            for j in range(3):
                last = nc.tensor.matmul(ps[:, j, 0:TB], ob["ones"][:], ob["acc"][:, j * TB:(j + 1) * TB],
                                        start=True, stop=True)
            last.then_inc(ou["summed"], 1)
            with pe.Fori(0, NCH) as it:
                for j in range(CH):
                    product(pe, j % 2, ffn_use(it, j), A, ready=(ou["n_lo"], 0) if j == 0 else None)
                for j in range(KT):
                    product(pe, j % 2, ffn_use(it, CH + j), O, kt=CH, ready=(ff["lo"], it * CH) if j == 0 else None)
            next_phase(pe, 12)
            for t in range(NT):
                k = t % 2
                if t >= 2:
                    pe.wait_ge(fin["y"][k], t // 2)
                for n in range(KT):
                    last = nc.tensor.transpose(ps[:, 2 * k + n // 4, (n % 4) * P:(n % 4 + 1) * P],
                                               H[:, n, t * P:(t + 1) * P], ident[:])
                last.then_inc(fin["turned"][k], 1)

        @block.scalar
        def _(act):
            act.wait_ge(consts_made, 1)
            with act.Fori(0, NLOOP) as it:
                for k in range(2):
                    norm_stats(act, bn, xn_sems, k, it)
                for k in range(2):
                    norm_hi(act, xn_sems, k, it, A, ds(it * (2 * P) + k * P, P))
            norm_stats(act, bn, xn_sems, 0, NLOOP)
            split_hi(act, 1, 0)
            norm_hi(act, xn_sems, 0, NLOOP, A, slice(QT * P, T))
            next_phase(act, 1)
            act.wait_ge(fs["b_in"], 16)
            act.wait_ge(gemm_over[1], 1)
            nc.scalar.activation(blocked(bf["x"][:], 3), ps[0:FH, 3:6, 0:TB], ACT.Identity,
                                 bias=bf["bf"][:]).then_inc(evacuated[1], 1)
            act.wait_ge(fs["neg"], 1)
            nc.scalar.activation(bf["e"][:], bf["e"][:], ACT.Exp).then_inc(fs["exp"], 1)
            act.wait_ge(fs["plus"], 1)
            nc.scalar.activation(bf["e"][:], bf["e"][:], ACT.Ln).then_inc(fs["ln"], 1)
            split_hi(act, 0, 0)
            next_phase(act, 2)
            with act.Fori(0, BT) as it:
                attend_act(act, fox, it, (QS, KS))
            next_phase(act, 3)
            sample_hi_keys(act, sfox, 0)
            with act.Fori(0, NB - 1) as i:
                sample_act(act, sfox, i, True)
            sample_act(act, sfox, NB - 1, False)
            next_phase(act, 4)
            merge_act(act, 0)
            next_phase(act, 5)
            act.wait_ge(po["w_in"], 16)
            nc.scalar.activation(pb["w"][0][:], pb["wraw"][:], ACT.Copy).then_inc(po["w_hi"], 1)
            split_hi(act, 1, uses["pool"][1])
            act.wait_ge(po["clear"], 1)
            for g in range(BT):
                k, c = g % 2, uses["pool"][g % 2] + g // 2
                act.wait_ge(gemm_over[k], c + 1)
                if g:
                    act.wait_ge(po["pooled"], g)
                    act.wait_ge(po["tail_t"], g)
                for j in range(3):
                    n = min(TB, SEQ - j * TB)
                    nc.scalar.activation(pb["u"][0][:, 16 + j * TB:16 + j * TB + n], ps[:, 3 * k + j, 0:n], ACT.Copy)
                rest = ps[:, 3 * k + 2, SEQ - 2 * TB:TB]
                nc.scalar.activation(pb["uf"][:, 0:P], ps[:, 3 * k + 2, SEQ - 2 * TB - P:SEQ - 2 * TB], ACT.Copy)
                nc.scalar.activation(pb["uf"][:, P:2 * P], rest, ACT.Copy).then_inc(po["u"], 1)
                seg = pb["u"][0][:, 16 + SEQ:UW].rearrange("p (b t) -> p b t", b=NB)
                nc.scalar.activation(seg[:, :, 16:16 + NQ], rest.rearrange("p (b q) -> p b q", b=NB),
                                     ACT.Copy).then_inc(evacuated[k], 1)
                if g + 2 < BT:
                    split_hi(act, k, c + 1)
                act.wait_ge(po["pooled"], g + 1)
                nc.scalar.activation(O[0][:, g, :], pb["pooled"][:], ACT.Copy).then_inc(po["d_hi"], 1)
            for g in range(BT):
                act.wait_ge(po["mix_over"], g + 1)
                if g == 0:
                    act.wait_ge(consts_in, 32)
                nc.scalar.activation(blocked(O[0][:, g, :], 3), pset(g % 2), ACT.Copy,
                                     scale=s_col[:, g:g + 1]).then_inc(po["o_hi"], 1)
            split_hi(act, 0, uses["merge1"][0])
            next_phase(act, 6)
            merge_act(act, 1)
            next_phase(act, 7)
            for t in range(MT):
                norm_stats(act, bm, xn_sems, t % 2, mem_use(t))
            for t in range(MT):
                norm_hi(act, xn_sems, t % 2, mem_use(t), ME, slice(t * P, (t + 1) * P))
            next_phase(act, 8)
            with act.Fori(0, BT) as it:
                attend_act(act, mem, it, (MQS,))
            next_phase(act, 9)
            sample_hi_keys(act, smem, 0)
            with act.Fori(0, NB - 1) as i:
                sample_act(act, smem, i, True)
            sample_act(act, smem, NB - 1, False)
            next_phase(act, 10)
            merge_act(act, 2)
            next_phase(act, 11)
            for t in range(KT):
                nc.scalar.activation(A[0][:, t, :], H[:, t, :], ACT.Copy).then_inc(ou["m_hi"], 1)
            with act.Fori(0, KT // 2) as it:
                for k in range(2):
                    act.wait_ge(ou[f"turned{k}"], it * 2 + 1)
                    act.wait_ge(evacuated[k], it + uses["out"][k])
                    nc.scalar.activation(ob["xt"][k][:, 0:SEQ], ps[:, 6:8, :].rearrange("p a c -> p (a c)"),
                                         ACT.Copy).then_inc(ou["xt"], 1)
                    split_hi(act, 1 - k, it + (uses["out"][1 - k] + k))
                    act.wait_ge(ou[f"turned{k}"], it * 2 + 2)
                    nc.scalar.activation(ob["xt"][k][:, SEQ:T], ps[:, 6, 0:P], ACT.Copy).then_inc(ou["xt"], 1)
                    act.wait_ge(evacuated[k], it + (uses["out"][k] + 1))
                    act.wait_ge(ou["acc"], it * 2 + k)
                    nc.scalar.activation(ob["sq"][:], H[:, it * 2 + k, :], ACT.Square).then_inc(ou["sq"], 1)
            act.wait_ge(ou["summed"], 1)
            nc.scalar.activation(blocked(ob["sq"][:], 3), pset(0), ACT.Sqrt, bias=eps_t[:],
                                 scale=1.0 / D).then_inc(ou["rooted"], 1)
            for t in range(KT):
                act.wait_ge(ou["hn"], t + 1)
                nc.scalar.activation(A[0][:, t, :], ob["hn" if t % 2 else "acc"][:], ACT.Copy).then_inc(ou["n_hi"], 1)

            def ffn_act(it, more):
                for j in range(CH):
                    split_hi(act, (j + 1) % 2, ffn_use(it, j + 1), KT if j + 1 < CH else CH)
                    act.wait_ge(gemm_over[j % 2], ffn_use(it, j) + 1)
                    act.wait_ge(ff["a"], it * CH + j)
                    nc.scalar.activation(blocked(fb["r"][:], 3), pset(j % 2), ACT.Relu).then_inc(evacuated[j % 2], 1)
                    act.wait_ge(ff["a"], it * CH + (j + 1))
                    if j == 0:
                        for x in range(2):
                            act.wait_ge(gemm_over[x], ffn_use(it, x))
                    nc.scalar.activation(O[0][:, j, :], fb["a"][:], ACT.Copy).then_inc(ff["hi"], 1)
                for j in range(1, KT):
                    split_hi(act, j % 2, ffn_use(it, CH + j), CH)
                if more:
                    split_hi(act, 0, ffn_use(it + 1, 0))

            with act.Fori(0, NCH - 1) as it:
                ffn_act(it, True)
            ffn_act(NCH - 1, False)
            next_phase(act, 12)
            for t in range(NT):
                k, n = t % 2, t // 2 + 1
                act.wait_ge(fin["turned"][k], n)
                st = yb["st"][k]
                nc.scalar.activation(yb["junk"][:], ps[:, 2 * k:2 * k + 2, :].rearrange("p a c -> p (a c)"),
                                     ACT.Square, accum_out=st[:, 0:1]).then_inc(fin["squared"][k], 1)
                act.wait_ge(fin["squared"][k], n)
                nc.scalar.activation(st[:, 1:2], st[:, 0:1], ACT.Sqrt, bias=eps_t[:],
                                     scale=1.0 / D).then_inc(fin["rooted"][k], 1)

        @block.vector
        def _(dve):
            dve.wait_ge(consts_made, 1)
            nc.vector.tensor_copy(ident_r[:], ident[:])
            dve.wait_ge(g_in["attn"], 16)
            with dve.Fori(0, NLOOP) as it:
                for k in range(2):
                    norm_scale(dve, bn, xn_sems, k, it)
                for k in range(2):
                    norm_lo(dve, xn_sems, k, it, A, ds(it * (2 * P) + k * P, P), xn_done)
            norm_scale(dve, bn, xn_sems, 0, NLOOP)
            split_lo(dve, 1, 0)
            norm_lo(dve, xn_sems, 0, NLOOP, A, slice(QT * P, T), xn_done)
            next_phase(dve, 1)
            nc.vector.memset(bf["zero"][:], 0.0).then_inc(fs["zero"], 1)
            dve.wait_ge(evacuated[1], 1)
            nc.vector.scalar_tensor_tensor(out=bf["e"][:], in0=bf["x"][:], scalar=-1.0, in1=bf["x"][:], op0=ALU.mult,
                                           op1=ALU.min).then_inc(fs["neg"], 1)
            dve.wait_ge(fs["exp"], 1)
            nc.vector.tensor_scalar(bf["e"][:], bf["e"][:], 1.0, None, ALU.add).then_inc(fs["plus"], 1)
            dve.wait_ge(fs["ln"], 1)
            nc.vector.scalar_tensor_tensor(out=bf["x"][:], in0=bf["x"][:], scalar=0.0, in1=bf["e"][:], op0=ALU.min,
                                           op1=ALU.subtract).then_inc(fs["logf"], 1)
            dve.wait_ge(fs["logf"], 1)
            nc.vector.tensor_scalar(bf["nl"][:], bf["x"][:], -1.0, None, ALU.mult).then_inc(fs["neg_logf"], 1)
            dve.wait_ge(fs["neg_logf"], 1)
            dve.wait_ge(fs["zero"], 1)
            nc.vector.tensor_tensor_scan(bf["c"][:], bf["nl"][:, 0:SEQ], bf["zero"][0:FH, :], 0.0, ALU.add,
                                         ALU.add).then_inc(fs["c"], 1)
            dve.wait_ge(fs["turned"], 1)
            nc.vector.tensor_copy(bf["tok"][:].rearrange("p t h -> p (t h)"), ps[:, 0, 0:NT * FH]).then_inc(fs["tok"], 1)
            dve.wait_ge(fs["cache_turned"], 1)
            nc.vector.tensor_scalar(bf["ext"][:, 0:PAST], ps[0:NB * FH, 1, 0:PAST], -1.0, None,
                                    ALU.mult).then_inc(fs["ext"], 1)
            dve.wait_ge(fs["ext"], 1)
            dve.wait_ge(fs["new_in"], 16 * NB)
            nc.vector.tensor_tensor_scan(bf["cs"][:], bf["ext"][:], bf["zero"][:, 0:PAST + NQ], 0.0, ALU.add,
                                         ALU.add).then_inc(fs["cs"], 1)
            dve.wait_ge(fs["masks"], 1)
            nc.vector.tensor_copy(causal_r[:], bf["cm"][:])
            nc.vector.tensor_reduce(rsel[:], bf["m3"][:].rearrange("p h q -> p q h"), AX_X, ALU.add)
            nc.vector.tensor_reduce(mask_new[:], bf["m4"][:].rearrange("p h q -> p q h"), AX_X,
                                    ALU.add).then_inc(fs["mask_sum"], 1)
            dve.wait_ge(fs["mask_sum"], 1)
            nc.vector.tensor_scalar(mask_new[:], mask_new[:], -1.0, BIG, ALU.add, ALU.mult)
            split_lo(dve, 0, 0)
            next_phase(dve, 2)
            with dve.Fori(0, BT) as it:
                attend_dve(dve, fox, it, (QS, KS))
            next_phase(dve, 3)

            def sample_first(a):
                first = a.base // NB + 1
                dve.wait_ge(a.s["block"], first)
                for x in range(2):
                    last = nc.vector.memset(a.b["qpad"][x][:].bitcast(F32), 0.0)
                last.then_inc(a.s["q_clear"], 1)
                dve.wait_ge(a.s["q_clear"], first)
                sample_lo_keys(dve, a, 0)
                sample_pad(dve, a, 0)

            sample_first(sfox)
            with dve.Fori(0, NB - 1) as i:
                sample_dve(dve, sfox, i, True)
            sample_dve(dve, sfox, NB - 1, False)
            next_phase(dve, 4)
            merge_dve(dve, 0)
            next_phase(dve, 5)
            for k in range(3):
                last = nc.vector.memset(pb["u"][k][:], 0.0)
            last.then_inc(po["clear"], 1)
            dve.wait_ge(po["clear"], 1)
            dve.wait_ge(po["w_hi"], 1)
            nc.vector.tensor_tensor(pb["w"][1][:], pb["wraw"][:], pb["w"][0][:].bitcast(F32),
                                    ALU.subtract).then_inc(po["w_lo"], 1)
            split_lo(dve, 1, uses["pool"][1])
            dve.wait_ge(po["hist_t"], 1)
            steps = 0
            for g in range(BT):
                k, c = g % 2, uses["pool"][g % 2] + g // 2
                raw = pb["u"][0]
                seg = raw[:, 16 + SEQ:UW].rearrange("p (b t) -> p b t", b=NB)
                nc.vector.tensor_copy(seg[:, :, 16 - HIST:16],
                                      ps[:, 6, g * P:g * P + NB * HIST].rearrange("p (b j) -> p b j", b=NB)
                                      ).then_inc(po["hist"], 1)
                dve.wait_ge(po["hist"], g + 1)
                dve.wait_ge(evacuated[k], c + 1)
                src = raw
                for x in range(g + 1):
                    dst, d = pb["u"][1 + x % 2], 2 ** x
                    nc.vector.tensor_tensor(dst[:, d:UW], src[:, d:UW], src[:, 0:UW - d], ALU.add).then_inc(po["step"], 1)
                    steps += 1
                    dve.wait_ge(po["step"], steps)
                    src = dst
                w = 2 ** (g + 1)
                nc.vector.tensor_tensor(pb["pooled"][:, 0:w], src[:, 16:16 + w], cnt_col[:, 0:w],
                                        ALU.mult).then_inc(po["first"], 1)
                nc.vector.scalar_tensor_tensor(out=pb["pooled"][:, w:SEQ], in0=src[:, 16 + w:16 + SEQ], scalar=1.0 / w,
                                               in1=raw[:, 16 + w:16 + SEQ], op0=ALU.mult, op1=ALU.subtract)
                nc.vector.scalar_tensor_tensor(
                    out=pb["pooled"][:, SEQ:T].rearrange("p (b q) -> p b q", b=NB),
                    in0=src[:, 16 + SEQ:UW].rearrange("p (b t) -> p b t", b=NB)[:, :, 16:16 + NQ], scalar=1.0 / w,
                    in1=seg[:, :, 16:16 + NQ], op0=ALU.mult, op1=ALU.subtract)
                dve.wait_ge(po["first"], g + 1)
                nc.vector.tensor_tensor(pb["pooled"][:, 0:w], pb["pooled"][:, 0:w], raw[:, 16:16 + w],
                                        ALU.subtract).then_inc(po["pooled"], 1)
                if g + 2 < BT:
                    split_lo(dve, k, c + 1)
                dve.wait_ge(po["tail_t"], g + 1)
                nc.vector.tensor_copy(pb["tail"][:, :, g * P:(g + 1) * P],
                                      ps[:, 7, 0:2 * P].rearrange("p (x c) -> p x c", x=2)).then_inc(po["tail"], 1)
                dve.wait_ge(po["pooled"], g + 1)
                dve.wait_ge(po["d_hi"], g + 1)
                nc.vector.tensor_tensor(O[1][:, g, :], pb["pooled"][:], O[0][:, g, :].bitcast(F32),
                                        ALU.subtract).then_inc(po["d_lo"], 1)
            for g in range(BT):
                dve.wait_ge(po["o_hi"], g + 1)
                nc.vector.scalar_tensor_tensor(out=blocked(O[1][:, g, :], 3), in0=pset(g % 2), scalar=s_col[:, g:g + 1],
                                               in1=blocked(O[0][:, g, :].bitcast(F32), 3), op0=ALU.mult,
                                               op1=ALU.subtract).then_inc(po["o_lo"], 1)
            split_lo(dve, 0, uses["merge1"][0])
            next_phase(dve, 6)
            merge_dve(dve, 1)
            next_phase(dve, 7)
            dve.wait_ge(g_in["mem"], 16)
            for t in range(MT):
                norm_scale(dve, bm, xn_sems, t % 2, mem_use(t))
            for t in range(MT):
                norm_lo(dve, xn_sems, t % 2, mem_use(t), ME, slice(t * P, (t + 1) * P), xn_done)
            next_phase(dve, 8)
            with dve.Fori(0, BT) as it:
                attend_dve(dve, mem, it, (MQS,))
            next_phase(dve, 9)
            sample_first(smem)
            with dve.Fori(0, NB - 1) as i:
                sample_dve(dve, smem, i, True)
            sample_dve(dve, smem, NB - 1, False)
            next_phase(dve, 10)
            merge_dve(dve, 2)
            next_phase(dve, 11)
            for t in range(KT):
                dve.wait_ge(ou["m_hi"], t + 1)
                nc.vector.tensor_tensor(A[1][:, t, :], H[:, t, :], A[0][:, t, :].bitcast(F32),
                                        ALU.subtract).then_inc(ou["m_lo"], 1)
            nc.vector.memset(ob["ones"][:], 1.0).then_inc(ou["ones"], 1)
            nc.vector.memset(ob["acc"][:], 0.0)
            with dve.Fori(0, KT // 2) as it:
                for k in range(2):
                    split_lo(dve, 1 - k, it + (uses["out"][1 - k] + k))
                    dve.wait_ge(gemm_over[k], it + (uses["out"][k] + 1))
                    dve.wait_ge(ou["xt"], it * 4 + (2 * k + 2))
                    nc.vector.tensor_tensor(blocked(H[:, it * 2 + k, :], 3), pset(k), blocked(ob["xt"][k][:], 3),
                                            ALU.add).then_inc(evacuated[k], 1)
                    dve.wait_ge(ou["sq"], it * 2 + (k + 1))
                    dve.wait_ge(ou["acc"], it * 2 + k)
                    nc.vector.tensor_tensor(ob["acc"][:], ob["acc"][:], ob["sq"][:], ALU.add).then_inc(ou["acc"], 1)
            dve.wait_ge(ou["rooted"], 1)
            nc.vector.reciprocal(ob["sq"][:], ob["sq"][:]).then_inc(ou["rstd"], 1)
            dve.wait_ge(ou["rstd"], 1)
            dve.wait_ge(consts_in, 32)

            def normalised(t):
                if t >= 2:
                    dve.wait_ge(ou["n_lo"], t - 1)
                nc.vector.scalar_tensor_tensor(out=ob["hn" if t % 2 else "acc"][:], in0=H[:, t, :],
                                               scalar=g_col[:, t:t + 1], in1=ob["sq"][:], op0=ALU.mult,
                                               op1=ALU.mult).then_inc(ou["hn"], 1)

            normalised(0)
            for t in range(KT):
                if t + 1 < KT:
                    normalised(t + 1)
                dve.wait_ge(ou["n_hi"], t + 1)
                dve.wait_ge(ou["hn"], t + 1)
                nc.vector.tensor_tensor(A[1][:, t, :], ob["hn" if t % 2 else "acc"][:], A[0][:, t, :].bitcast(F32),
                                        ALU.subtract).then_inc(ou["n_lo"], 1)

            def ffn_dve(it, more):
                for j in range(CH):
                    split_lo(dve, (j + 1) % 2, ffn_use(it, j + 1), KT if j + 1 < CH else CH)
                    dve.wait_ge(evacuated[j % 2], ffn_use(it, j) + 1)
                    dve.wait_ge(ff["lo"], it * CH + j)
                    nc.vector.tensor_tensor(fb["a"][:], fb["r"][:], fb["r"][:], ALU.mult).then_inc(ff["a"], 1)
                    dve.wait_ge(ff["hi"], it * CH + (j + 1))
                    nc.vector.tensor_tensor(O[1][:, j, :], fb["a"][:], O[0][:, j, :].bitcast(F32),
                                            ALU.subtract).then_inc(ff["lo"], 1)
                for j in range(KT):
                    if j + 1 < KT:
                        split_lo(dve, (j + 1) % 2, ffn_use(it, CH + j + 1), CH)
                    elif more:
                        split_lo(dve, 0, ffn_use(it + 1, 0))
                    dve.wait_ge(gemm_over[j % 2], ffn_use(it, CH + j) + 1)
                    nc.vector.tensor_tensor(blocked(H[:, j, :], 3), pset(j % 2), blocked(H[:, j, :], 3),
                                            ALU.add).then_inc(evacuated[j % 2], 1)

            with dve.Fori(0, NCH - 1) as it:
                ffn_dve(it, True)
            ffn_dve(NCH - 1, False)
            next_phase(dve, 12)
            dve.wait_ge(g_in["fin"], 16)
            for t in range(NT):
                k, n = t % 2, t // 2 + 1
                st = yb["st"][k]
                dve.wait_ge(fin["rooted"][k], n)
                nc.vector.reciprocal(st[:, 2:3], st[:, 1:2]).then_inc(fin["recip"][k], 1)
                dve.wait_ge(fin["recip"][k], n)
                if n > 1:
                    dve.wait_ge(fin["stored"][k], 16 * (n - 1))
                nc.vector.scalar_tensor_tensor(out=yb["y"][k][:], scalar=st[:, 2:3], in1=yb["g"][:],
                                               in0=ps[:, 2 * k:2 * k + 2, :].rearrange("p a c -> p (a c)"),
                                               op0=ALU.mult, op1=ALU.mult).then_inc(fin["y"][k], 1)


_INS = ['x_prompt', 'x_sample', 'mem_prompt', 'cache_fox_k', 'cache_fox_v', 'cache_fox_logf', 'cache_pool',
        'cache_mem_k', 'cache_mem_v', 'g_attn', 'w_in', 'b_f', 'w_pool', 's_pool', 'g_mem', 'w_mkv', 'w_br_fox',
        'w_br_pool', 'w_br_mem', 'w_out', 'g_mlp', 'w_up', 'w_down', 'g_final']
_OUTS = [(1, 1024, 1024), (8, 16, 1024), (1, 1, 1024, 8, 64), (1, 1, 1024, 8, 64), (1, 1, 1024, 8), (1, 1, 15, 512),
         (1, 1, 256, 4, 128), (1, 1, 256, 4, 128), (1, 8, 16, 8, 64), (1, 8, 16, 8, 64), (1, 8, 16, 8), (1, 8, 15, 512)]


def kernel(**inputs):
    import numpy as _np
    import concourse.bacc as _bacc
    from concourse import mybir as _mybir
    from concourse.bass_utils import run_bass_kernel_spmd as _run

    nc = _bacc.Bacc("TRN2", target_bir_lowering=False, num_devices=1, dynamic_dma_scratch_size=64)
    arrays, args = {}, []
    for name in _INS:
        a = _np.ascontiguousarray(inputs[name])
        arrays[f"in_{name}_dram"] = a
        args.append(nc.dram_tensor(f"in_{name}_dram", a.shape, _mybir.dt.from_np(a.dtype), kind="ExternalInput").ap())
    for i, shape in enumerate(_OUTS):
        args.append(nc.dram_tensor(f"out_{i}_dram", shape, _mybir.dt.float32, kind="ExternalOutput").ap())
    encoder_program(nc, *args)
    r = _run(nc, [arrays], core_ids=[0])
    return tuple(r.results[0][f"out_{i}_dram"] for i in range(len(_OUTS)))
```
